# Optimizing a Trainium2 kernel written in Bass

```python
import jax, jax.numpy as jnp
from jax import lax
import numpy as np

D_MODEL = 1024
BATCH = 1
SEQ = 1024
DEPTH = 1

CHUNK = 64
MIX_WIDTH = D_MODEL
CONV_WIDTH = MIX_WIDTH // 2
POOL_WIDTH = MIX_WIDTH - CONV_WIDTH
CONV_HEADS = 8
CONV_K = 3
POOL_WINDOWS = (2, 4, 8, 16)
POOL_GROUPS = len(POOL_WINDOWS)
POOL_GROUP_WIDTH = POOL_WIDTH // POOL_GROUPS
IN_PROJ_WIDTH = 3 * CONV_WIDTH + POOL_WIDTH
D_FF = 4 * D_MODEL
EPS = 1e-6

kernel_name = "hybrid_shortconv_multipool_block"

def rmsnorm(x, g):
    xf = x.astype(jnp.float32)
    r = lax.rsqrt(jnp.mean(xf * xf, axis=-1, keepdims=True) + EPS)
    return (xf * r).astype(x.dtype) * g

def short_gated_conv(h, gate_b, gate_c, conv_w):
    s = h.shape[1]
    z = gate_c * h
    zp = jnp.pad(z, ((0, 0), (CONV_K - 1, 0), (0, 0)))
    conv = conv_w[0] * zp[:, 0:s] + conv_w[1] * zp[:, 1:s + 1] + conv_w[2] * zp[:, 2:s + 2]
    return gate_b * conv

def multiscale_causal_pool(v, pool_w, pool_scale):
    b, s, _ = v.shape
    cs = jnp.cumsum(v.astype(jnp.float32), axis=1)
    pos = jnp.arange(s, dtype=jnp.float32)
    outs = []
    for gi, w in enumerate(POOL_WINDOWS):
        lo, hi = gi * POOL_GROUP_WIDTH, (gi + 1) * POOL_GROUP_WIDTH
        cs_g = cs[..., lo:hi]
        cs_shift = jnp.pad(cs_g, ((0, 0), (w, 0), (0, 0)))[:, :s]
        count = jnp.minimum(pos + 1.0, float(w))[None, :, None]
        mean = (cs_g - cs_shift) / count
        outs.append((mean - v[..., lo:hi].astype(jnp.float32)).astype(v.dtype))
    u = jnp.stack(outs, axis=2)
    y = jnp.einsum('bsgc,gcd->bsgd', u, pool_w)
    return y.reshape(b, s, POOL_WIDTH) * pool_scale

def setup_inputs(seed: int = 0) -> dict:
    key = jax.random.key(seed)
    ks = jax.random.split(key, 12)
    f32 = jnp.float32
    x = jax.random.normal(ks[0], (BATCH, SEQ, D_MODEL), f32)
    norm_mix_g = 1.0 + 0.05 * jax.random.normal(ks[1], (DEPTH, D_MODEL), f32)
    w_in = jax.random.normal(ks[2], (DEPTH, D_MODEL, IN_PROJ_WIDTH), f32) * D_MODEL ** -0.5
    conv_w = jax.random.normal(ks[3], (DEPTH, CONV_K, CONV_WIDTH), f32) * CONV_K ** -0.5
    pool_w = jax.random.normal(ks[4], (DEPTH, POOL_GROUPS, POOL_GROUP_WIDTH, POOL_GROUP_WIDTH), f32) * POOL_GROUP_WIDTH ** -0.5
    pool_scale = 1.0 + 0.1 * jax.random.normal(ks[5], (DEPTH, POOL_WIDTH), f32)
    w_out = jax.random.normal(ks[6], (DEPTH, MIX_WIDTH, D_MODEL), f32) * MIX_WIDTH ** -0.5
    norm_mlp_g = 1.0 + 0.05 * jax.random.normal(ks[7], (DEPTH, D_MODEL), f32)
    w_ff1 = jax.random.normal(ks[8], (DEPTH, D_MODEL, D_FF), f32) * D_MODEL ** -0.5
    w_ff2 = jax.random.normal(ks[9], (DEPTH, D_FF, D_MODEL), f32) * D_FF ** -0.5
    norm_final_g = 1.0 + 0.05 * jax.random.normal(ks[10], (D_MODEL,), f32)
    return {"x": x, "norm_mix_g": norm_mix_g, "w_in": w_in, "conv_w": conv_w,
            "pool_w": pool_w, "pool_scale": pool_scale, "w_out": w_out,
            "norm_mlp_g": norm_mlp_g, "w_ff1": w_ff1, "w_ff2": w_ff2,
            "norm_final_g": norm_final_g}

def reference(x, norm_mix_g, w_in, conv_w, pool_w, pool_scale, w_out,
              norm_mlp_g, w_ff1, w_ff2, norm_final_g):
    for l in range(DEPTH):
        xn = rmsnorm(x, norm_mix_g[l])
        proj = jnp.einsum('bsd,de->bse', xn, w_in[l])
        h = proj[..., 0:CONV_WIDTH]
        gate_b = proj[..., CONV_WIDTH:2 * CONV_WIDTH]
        gate_c = proj[..., 2 * CONV_WIDTH:3 * CONV_WIDTH]
        v = proj[..., 3 * CONV_WIDTH:]
        y_conv = short_gated_conv(h, gate_b, gate_c, conv_w[l])
        y_pool = multiscale_causal_pool(v, pool_w[l], pool_scale[l])
        y = jnp.concatenate([y_conv, y_pool], axis=-1)
        x = x + jnp.einsum('bse,ed->bsd', y, w_out[l])
        xn = rmsnorm(x, norm_mlp_g[l])
        hid = jnp.square(jax.nn.relu(jnp.einsum('bsd,df->bsf', xn, w_ff1[l])))
        x = x + jnp.einsum('bsf,fd->bsd', hid, w_ff2[l])
    return rmsnorm(x, norm_final_g)


_drawn_inputs = setup_inputs


def setup_inputs(seed=0):
    import zlib

    import numpy as np

    out = dict(_drawn_inputs(seed))
    spreads = {}
    factors = {}
    for name, (base, spread) in spreads.items():
        noise = np.random.default_rng([zlib.crc32(name.encode()), seed]).standard_normal(out[name].shape)
        drawn = base * np.exp(spread * noise) if base else spread * noise
        out[name] = __import__('jax').numpy.asarray(drawn.astype(out[name].dtype))
    for name, factor in factors.items():
        out[name] = (out[name] * factor).astype(out[name].dtype)
    return out
```

```python
from contextlib import ExitStack

import concourse.bass as bass
from concourse import mybir

P = 128
T = 1024
D = 1024
HALF = 512
TILES = T // P
DB = D // P
KC = 4
D_FF = 4 * D
CHUNKS = D_FF // (KC * P)
CONV = 512
WINDOWS = (2, 4, 8, 16)
TAPS = 3
EPS = 1e-6
PAD = 16
STAGES = 4
UP_SLOTS = 2

MIX_UNITS = [("v", 0), ("v", 1), ("v", 2), ("v", 3), ("h", 0), ("pw", 0), ("c", 0), ("b", 0),
             ("h", 1), ("c", 1), ("b", 1), ("h", 2), ("c", 2), ("b", 2), ("h", 3), ("c", 3), ("b", 3)]
MIX_COLUMN = {"h": 0, "b": CONV, "c": 2 * CONV, "v": 3 * CONV}
MIX_LOADS = [("v", 0), ("v", 1), ("v", 2), ("out", 4), ("v", 3), ("out", 5), ("h", 0), ("out", 6),
             ("pw", 0), ("out", 7), ("c", 0), ("b", 0), ("h", 1), ("c", 1), ("out", 0),
             ("b", 1), ("h", 2), ("out", 1), ("c", 2), ("out", 2),
             ("b", 2), ("h", 3), ("out", 3), ("c", 3), ("b", 3)]
CHUNK_LOADS = [("ff1", 0), ("ff1", 1), ("ff2", 0), ("ff1", 2), ("ff2", 1), ("ff1", 3), ("ff2", 2), ("ff2", 3)]
N_MIX_LOADS = len(MIX_LOADS)
N_CHUNK_LOADS = len(CHUNK_LOADS)
assert N_CHUNK_LOADS % STAGES == 0

UP_BANKS, DOWN_BANKS = 2, 4
G_PAIR = 0
G_PW = 4
G_POOL = G_PW + 8
G_CONV = G_POOL + 16
G_MLP = G_CONV + 16
UP_ORDER = [u for u in MIX_UNITS if u not in (("v", 0), ("v", 1), ("pw", 0))]
S_MLP = 2 * len(UP_ORDER)
ORDER_FIRST = [(0, 0), (1, 0), (0, 1), (1, 1), (2, 0), (2, 1), (3, 0), (3, 1)]
ORDER_LATER = [(j, h) for j in range(KC) for h in range(2)]
LAST_OF_UNIT = {order_id: {j: max(i for i, (u, _) in enumerate(order) if u == j) for j in range(KC)}
                for order_id, order in (("first", ORDER_FIRST), ("later", ORDER_LATER))}
A_MLP = 16


def up_group(unit, half):
    return 2 * UP_ORDER.index(unit) + half


def load_number(c, pos):
    return N_MIX_LOADS + N_CHUNK_LOADS * c + pos


def build(nc, x, norm_mix_g, w_in, conv_w, pool_w, pool_scale, w_out, norm_mlp_g, w_ff1, w_ff2,
          norm_final_g, out):
    F32, F32R = mybir.dt.float32, mybir.dt.float32r
    ACT, ALU = mybir.ActivationFunctionType, mybir.AluOpType

    x_tiles = x[0].rearrange("(m p) d -> m p d", p=P)
    out_tiles = out[0].rearrange("(m p) d -> m p d", p=P)
    w_in_cols = w_in[0].rearrange("(k p) e -> p k e", p=P)
    w_ff1_cols = w_ff1[0].rearrange("(k p) e -> p k e", p=P)

    with ExitStack() as ctx:
        def sb(name, shape, dt=F32):
            return ctx.enter_context(nc.sbuf_tensor(name, shape, dt))

        def sem(name):
            return ctx.enter_context(nc.semaphore(name))

        stream = sb("stream", [P, TILES, D])
        xt_hi = sb("xt_hi", [P, DB, T], F32R)
        xt_lo = sb("xt_lo", [P, DB, T], F32R)
        act_hi = sb("act_hi", [P, KC, T], F32R)
        act_lo = sb("act_lo", [P, KC, T], F32R)
        down_hi = sb("down_hi", [P, KC, D], F32R)
        down_lo = sb("down_lo", [P, KC, D], F32R)
        up_hi = sb("up_hi", [P, UP_SLOTS, D], F32R)
        up_lo = sb("up_lo", [P, UP_SLOTS, D], F32R)
        raw = sb("raw", [P, STAGES, D])
        scratch = sb("scratch", [P, 3, PAD + T])
        ident = sb("ident", [P, P])
        counts = sb("counts", [P, WINDOWS[-1]])
        head = sb("head", [P, WINDOWS[-1]])
        rows = sb("rows", [16, P])
        cols = sb("cols", [P, 16])
        sumsq = sb("sumsq", [P, 3 * TILES])
        meansq = sb("meansq", [P, 3 * TILES])
        root = sb("root", [P, 3 * TILES])
        guess = sb("guess", [P, 3 * TILES])
        newton = sb("newton", [P, 2, 3 * TILES])
        rstd = sb("rstd", [P, 3 * TILES])
        psum = [ctx.enter_context(nc.psum_tensor(f"bank{b}", [P, HALF], F32)) for b in range(8)]

        row = [scratch[:, i, PAD:PAD + T] for i in range(3)]
        gain = row[2]

        x_landed = [sem(f"x_landed{m}") for m in range(TILES)]
        raw_landed = [sem(f"raw_landed{s}") for s in range(STAGES)]
        gain_landed, rows_landed, stored = sem("gain_landed"), sem("rows_landed"), sem("stored")
        ident_zeroed, ident_ready, consts_ready = sem("ident_zeroed"), sem("ident_ready"), sem("consts_ready")
        cols_transposed, cols_ready = sem("cols_transposed"), sem("cols_ready")
        squared, mean_ready, root_ready = sem("squared"), sem("mean_ready"), sem("root_ready")
        newton_step, rstd_ready, normed = sem("newton_step"), sem("rstd_ready"), sem("normed")
        transposed, xt_hi_ready, xt_ready = sem("transposed"), sem("xt_hi_ready"), sem("xt_ready")
        w_hi_ready, w_ready = sem("w_hi_ready"), sem("w_ready")
        up_done, down_done = sem("up_done"), sem("down_done")
        bank_read = [sem(f"bank_read{b}") for b in range(UP_BANKS + DOWN_BANKS)]
        window_added, head_ready, pooled = sem("window_added"), sem("head_ready"), sem("pooled")
        u_hi_ready, u_ready = sem("u_hi_ready"), sem("u_ready")
        tap_done, y_ready = sem("tap_done"), sem("y_ready")
        squared_relu = sem("squared_relu")
        act_hi_ready, act_ready = sem("act_hi_ready"), sem("act_ready")

        def up_bank(s):
            return s % UP_BANKS

        def down_bank(g):
            return UP_BANKS + g % DOWN_BANKS

        def wait_group(eng, kind, base, step, c=0):
            eng.wait_ge(up_done if kind == "up" else down_done, base + 1 + step * c)

        def wait_bank_read(eng, kind, base, step, c=0):
            banks, bank = (UP_BANKS, up_bank) if kind == "up" else (DOWN_BANKS, down_bank)
            eng.wait_ge(bank_read[bank(base)], base // banks + 1 + step // banks * c)

        def wait_unit(eng, unit):
            if unit == ("pw", 0):
                wait_group(eng, "down", G_PW + 7, 0)
            elif unit in UP_ORDER:
                wait_group(eng, "up", up_group(unit, 1), 0)
            else:
                wait_group(eng, "down", G_PAIR + 2 + unit[1], 0)

        def split_target(what, c, u=None):
            kind, j = what
            if kind in ("out", "ff2"):
                return down_hi[:, j % KC, :], down_lo[:, j % KC, :], D
            if kind == "ff1":
                slot = (len(MIX_UNITS) + j) % UP_SLOTS
            else:
                slot = MIX_UNITS.index(what) % UP_SLOTS
            width = KC * P if kind == "pw" else D
            return up_hi[:, slot, 0:width], up_lo[:, slot, 0:width], width

        block = ctx.enter_context(nc.Block())

        @block.sync
        def _(sp):
            def load(n0, per_chunk, what, c):
                kind, j = what
                slot = n0 % STAGES
                if n0 >= STAGES:
                    sp.wait_ge(w_ready, n0 - STAGES + 1 + per_chunk * c)
                dst = raw[:, slot, :]
                if kind == "out":
                    src = w_out[0, j * P:(j + 1) * P, :]
                elif kind == "ff2":
                    src = w_ff2[0, bass.ds(c * (KC * P) + j * P, P), :]
                elif kind == "ff1":
                    dst = dst.rearrange("p (k e) -> p k e", e=P)
                    src = w_ff1_cols[:, :, bass.ds(c * (KC * P) + j * P, P)]
                elif kind == "pw":
                    dst = dst[:, 0:KC * P].rearrange("p (g e) -> p g e", e=P)
                    src = pool_w[0].rearrange("g c e -> c g e")
                else:
                    e0 = MIX_COLUMN[kind] + j * P
                    dst = dst.rearrange("p (k e) -> p k e", e=P)
                    src = w_in_cols[:, :, e0:e0 + P]
                sp.dma_start(dst, src).then_inc(raw_landed[slot], 16)

            def load_gain(g):
                sp.dma_start(gain, g.partition_broadcast(P)).then_inc(gain_landed, 16)

            sp.dma_start(stream[:, 0, :], x_tiles[0]).then_inc(x_landed[0], 16)
            load_gain(norm_mix_g[0])
            for m in range(1, 4):
                sp.dma_start(stream[:, m, :], x_tiles[m]).then_inc(x_landed[m], 16)
            load(0, 0, MIX_LOADS[0], 0)
            for m in range(4, TILES):
                sp.dma_start(stream[:, m, :], x_tiles[m]).then_inc(x_landed[m], 16)
            load(1, 0, MIX_LOADS[1], 0)
            sp.dma_start(rows[0:12, :], conv_w[0].rearrange("t (j p) -> (t j) p", p=P)).then_inc(rows_landed, 16)
            sp.dma_start(rows[12:16, :], pool_scale[0].rearrange("(j p) -> j p", p=P)).then_inc(rows_landed, 16)
            for n in range(2, N_MIX_LOADS):
                load(n, 0, MIX_LOADS[n], 0)
                if MIX_LOADS[n] == ("c", 1):
                    sp.wait_ge(u_ready, KC)
                    load_gain(norm_mlp_g[0])
            for pos in range(N_CHUNK_LOADS):
                load(load_number(0, pos), 0, CHUNK_LOADS[pos], 0)
            sp.wait_ge(normed, 2 * TILES)
            load_gain(norm_final_g)
            with sp.Fori(1, CHUNKS) as c:
                for pos in range(N_CHUNK_LOADS):
                    load(load_number(0, pos), N_CHUNK_LOADS, CHUNK_LOADS[pos], c)
            for m in range(TILES):
                sp.wait_ge(normed, 2 * TILES + m + 1)
                sp.dma_start(out_tiles[m], stream[:, m, :]).then_inc(stored, 16)
            sp.wait_ge(stored, 16 * TILES)

        @block.gpsimd
        def _(pool):
            nc.gpsimd.memset(ident[:, :], 0.0).then_inc(ident_zeroed, 1)
            pool.wait_ge(ident_zeroed, 1)
            nc.gpsimd.affine_select(out=ident[:, :], in_=ident[:, :], compare_op=ALU.not_equal, fill=1.0,
                                    base=0, pattern=[[-1, P]], channel_multiplier=1).then_inc(ident_ready, 1)
            nc.gpsimd.memset(scratch[:, :, 0:PAD], 0.0).then_inc(consts_ready, 1)
            for t in range(WINDOWS[-1]):
                nc.gpsimd.memset(counts[:, t:t + 1], 1.0 / (t + 1)).then_inc(consts_ready, 1)

        N_CONSTS = 1 + WINDOWS[-1]

        @block.scalar
        def _(act):
            def split_hi(what, n0, per_chunk=0, c=0):
                hi, _, width = split_target(what, c)
                act.wait_ge(raw_landed[n0 % STAGES], 16 * (n0 // STAGES + 1) + 16 * (per_chunk // STAGES) * c)
                nc.scalar.activation(hi, raw[:, n0 % STAGES, 0:width], ACT.Copy).then_inc(w_hi_ready, 1)

            def split_mix_hi(what):
                n = MIX_LOADS.index(what)
                if what[0] != "out":
                    u = MIX_UNITS.index(what)
                    if u >= UP_SLOTS:
                        wait_unit(act, MIX_UNITS[u - UP_SLOTS])
                elif what[1] < KC:
                    wait_group(act, "down", G_CONV - 1, 0)
                split_hi(what, n)

            def root_mean_square(norm, m):
                i = norm * TILES + m
                if norm == 0:
                    act.wait_ge(x_landed[m], 16)
                    if m >= 2:
                        act.wait_ge(transposed, 2 * (m - 1))
                elif norm == 1:
                    wait_bank_read(act, "down", G_CONV + 2 * m, 0)
                    wait_bank_read(act, "down", G_CONV + 2 * m + 1, 0)
                    if m >= 2:
                        act.wait_ge(transposed, 2 * TILES + 2 * (m - 1))
                else:
                    g = G_MLP + 16 * (CHUNKS - 1)
                    wait_bank_read(act, "down", g + 2 * m, 0)
                    wait_bank_read(act, "down", g + 2 * m + 1, 0)
                nc.scalar.activation(row[m % 2], stream[:, m, :], ACT.Square,
                                     accum_out=sumsq[:, i:i + 1]).then_inc(squared, 1)
                act.wait_ge(mean_ready, i + 1)
                nc.scalar.activation(root[:, i:i + 1], meansq[:, i:i + 1], ACT.Sqrt).then_inc(root_ready, 1)

            def transpose_hi(norm, m):
                for q in range(2):
                    n = 2 * (norm * TILES + m) + q
                    act.wait_ge(transposed, n + 1)
                    nc.scalar.activation(xt_hi[:, 4 * q:4 * q + 4, m * P:(m + 1) * P],
                                         psum[6 + q][:, :].rearrange("p (k t) -> p k t", t=P),
                                         ACT.Copy).then_inc(xt_hi_ready, 1)

            for m in range(TILES):
                root_mean_square(0, m)
                if m >= 1:
                    transpose_hi(0, m - 1)
                if m == 3:
                    split_mix_hi(("v", 0))
                if m == 5:
                    split_mix_hi(("v", 1))
            transpose_hi(0, TILES - 1)
            act.wait_ge(cols_transposed, 1)
            nc.scalar.activation(cols[:, :], psum[0][:, 0:16], ACT.Copy).then_inc(cols_ready, 1)

            for j in range(KC):
                if j == 0:
                    split_mix_hi(("v", 2))
                    act.wait_ge(normed, TILES)
                    act.wait_ge(transposed, 2 * TILES)
                else:
                    act.wait_ge(pooled, j)
                for half in range(2):
                    kind, g = ("down", G_PAIR + 2 * half + j) if j < 2 else ("up", up_group(("v", j), half))
                    bank = down_bank(g) if j < 2 else up_bank(g)
                    wait_group(act, kind, g, 0)
                    nc.scalar.activation(row[0][:, half * HALF:(half + 1) * HALF], psum[bank][:, :],
                                         ACT.Copy).then_inc(bank_read[bank], 1)
                if j >= 1:
                    split_mix_hi([("v", 3), ("h", 0), ("pw", 0)][j - 1])
                split_mix_hi(("out", KC + j))
                act.wait_ge(pooled, j + 1)
                nc.scalar.activation(act_hi[:, j, :], row[1 + j % 2], ACT.Copy).then_inc(u_hi_ready, 1)

            for j in range(KC):
                if j > 0:
                    act.wait_ge(act_ready, 8 + 2 * j)
                for half in range(2):
                    s = up_group(("h", j), half)
                    wait_group(act, "up", s, 0)
                    nc.scalar.activation(row[0][:, half * HALF:(half + 1) * HALF], psum[up_bank(s)][:, :],
                                         ACT.Copy).then_inc(bank_read[up_bank(s)], 1)
                if j == 0:
                    split_mix_hi(("c", 0))
                    for i in range(8):
                        g = G_PW + i
                        wait_group(act, "down", g, 0)
                        nc.scalar.activation(act_hi[:, i // 2, (i % 2) * HALF:(i % 2 + 1) * HALF],
                                             psum[down_bank(g)][:, :], ACT.Copy,
                                             scale=cols[:, 12 + i // 2:13 + i // 2]).then_inc(act_hi_ready, 1)
                split_mix_hi(("b", j))
                if j < 3:
                    split_mix_hi(("h", j + 1))
                    if j >= 1:
                        split_mix_hi(("out", 2 * j - 1))
                else:
                    wait_unit(act, ("c", 3))
                    split_hi(CHUNK_LOADS[0], load_number(0, 0))
                for half in range(2):
                    act.wait_ge(y_ready, 2 * j + half + 1)
                    nc.scalar.activation(act_hi[:, j, half * HALF:(half + 1) * HALF],
                                         row[0][:, half * HALF:(half + 1) * HALF],
                                         ACT.Copy).then_inc(act_hi_ready, 1)
                if j < 3:
                    split_mix_hi(("c", j + 1))
                    if j < 2:
                        split_mix_hi(("out", 2 * j))
                else:
                    wait_unit(act, ("b", 3))
                    split_hi(CHUNK_LOADS[1], load_number(0, 1))

            for m in range(TILES):
                root_mean_square(1, m)
                if m >= 2:
                    transpose_hi(1, m - 2)

            def relu(order, c, i):
                k, half = order[i]
                act.wait_ge(squared_relu, i - 1 + 8 * c) if not (isinstance(c, int) and c == 0 and i < 2) else None
                wait_group(act, "up", S_MLP + i, 8, c)
                r = row[0][:, (i % 2) * HALF:(i % 2 + 1) * HALF]
                nc.scalar.activation(r, psum[up_bank(i)][:, :], ACT.Relu).then_inc(bank_read[up_bank(i)], 1)
                wait_bank_read(act, "up", S_MLP + i, 8, c)
                nc.scalar.activation(act_hi[:, k, half * HALF:(half + 1) * HALF], r,
                                     ACT.Square).then_inc(act_hi_ready, 1)

            def split_ff1(j, c, order_id):
                wait_group(act, "up", S_MLP + LAST_OF_UNIT[order_id][j - 2], 8, c)
                pos = CHUNK_LOADS.index(("ff1", j))
                split_hi(("ff1", j), load_number(0, pos), N_CHUNK_LOADS, c)

            def split_ff2(k, c):
                pos = CHUNK_LOADS.index(("ff2", k))
                split_hi(("ff2", k), load_number(0, pos), N_CHUNK_LOADS, c)

            def split_next_ff1(c):
                for j in range(2):
                    wait_group(act, "up", S_MLP + LAST_OF_UNIT["later"][2 + j], 8, c)
                    split_hi(("ff1", j), load_number(1, j), N_CHUNK_LOADS, c)

            transpose_hi(1, TILES - 2)
            transpose_hi(1, TILES - 1)
            wait_group(act, "down", G_MLP - 1, 0)
            relu(ORDER_FIRST, 0, 0)
            split_ff2(0, 0)
            relu(ORDER_FIRST, 0, 1)
            relu(ORDER_FIRST, 0, 2)
            split_ff1(2, 0, "first")
            relu(ORDER_FIRST, 0, 3)
            split_ff2(1, 0)
            split_ff1(3, 0, "first")
            relu(ORDER_FIRST, 0, 4)
            split_ff2(2, 0)
            split_ff2(3, 0)
            for i in range(5, 8):
                relu(ORDER_FIRST, 0, i)
            split_next_ff1(0)

            def chunk(c):
                wait_group(act, "down", G_MLP - 1, 16, c)
                for j in range(KC):
                    if j in (1, 2):
                        split_ff1(j + 1, c, "later")
                    if j == 0:
                        split_ff2(0, c)
                    elif j < 3:
                        split_ff2(j, c)
                    else:
                        split_ff2(3, c)
                    relu(ORDER_LATER, c, 2 * j)
                    relu(ORDER_LATER, c, 2 * j + 1)

            with act.Fori(1, CHUNKS - 1) as c:
                chunk(c)
                split_next_ff1(c)
            chunk(CHUNKS - 1)
            for m in range(TILES):
                root_mean_square(2, m)

        @block.vector
        def _(dve):
            def split_lo(what, n0, per_chunk=0, c=0):
                hi, lo, width = split_target(what, c)
                dve.wait_ge(w_hi_ready, n0 + 1 + per_chunk * c)
                nc.vector.tensor_tensor(lo, raw[:, n0 % STAGES, 0:width], hi.bitcast(F32),
                                        ALU.subtract).then_inc(w_ready, 1)

            def split_mix_lo(what):
                split_lo(what, MIX_LOADS.index(what))

            def normalise(norm, m):
                i = norm * TILES + m
                at = slice(i, i + 1)
                dve.wait_ge(squared, i + 1)
                nc.vector.tensor_scalar(meansq[:, at], sumsq[:, at], 1.0 / D, EPS, ALU.mult,
                                        ALU.add).then_inc(mean_ready, 1)
                dve.wait_ge(root_ready, i + 1)
                nc.vector.reciprocal(guess[:, at], root[:, at]).then_inc(newton_step, 1)
                dve.wait_ge(newton_step, 3 * i + 1)
                nc.vector.scalar_tensor_tensor(newton[:, 0, at], meansq[:, at], guess[:, at], guess[:, at],
                                               ALU.mult, ALU.mult).then_inc(newton_step, 1)
                dve.wait_ge(newton_step, 3 * i + 2)
                nc.vector.tensor_scalar(newton[:, 1, at], newton[:, 0, at], -0.5, 1.5, ALU.mult,
                                        ALU.add).then_inc(newton_step, 1)
                dve.wait_ge(newton_step, 3 * i + 3)
                nc.vector.tensor_tensor(rstd[:, at], guess[:, at], newton[:, 1, at],
                                        ALU.mult).then_inc(rstd_ready, 1)
                dve.wait_ge(rstd_ready, i + 1)
                if m == 0:
                    dve.wait_ge(gain_landed, 16 * (norm + 1))
                dst = stream[:, m, :] if norm == 2 else row[m % 2]
                nc.vector.scalar_tensor_tensor(dst, stream[:, m, :], rstd[:, at], gain,
                                               ALU.mult, ALU.mult).then_inc(normed, 1)

            def transpose_lo(norm, m):
                for q in range(2):
                    n = 2 * (norm * TILES + m) + q
                    hi = xt_hi[:, 4 * q:4 * q + 4, m * P:(m + 1) * P]
                    dve.wait_ge(xt_hi_ready, n + 1)
                    nc.vector.tensor_tensor(xt_lo[:, 4 * q:4 * q + 4, m * P:(m + 1) * P],
                                            psum[6 + q][:, :].rearrange("p (k t) -> p k t", t=P),
                                            hi.bitcast(F32), ALU.subtract).then_inc(xt_ready, 1)

            def add_group(base, i, c=0, first=False):
                g = base + i
                dst = stream[:, i // 2, (i % 2) * HALF:(i % 2 + 1) * HALF]
                if not first:
                    wait_bank_read(dve, "down", g - 16, 16, c)
                wait_group(dve, "down", g, 16, c)
                nc.vector.tensor_tensor(dst, psum[down_bank(g)][:, :], dst,
                                        ALU.add).then_inc(bank_read[down_bank(g)], 1)

            for m in range(TILES):
                normalise(0, m)
                if m >= 1:
                    transpose_lo(0, m - 1)
                if m == 3:
                    split_mix_lo(("v", 0))
                if m == 5:
                    split_mix_lo(("v", 1))
            transpose_lo(0, TILES - 1)

            dve.wait_ge(consts_ready, N_CONSTS)
            added = 0
            for j in range(KC):
                if j == 0:
                    split_mix_lo(("v", 2))
                w = WINDOWS[j]
                for half in range(2):
                    if j < 2:
                        wait_bank_read(dve, "down", G_PAIR + 2 * half + j, 0)
                    else:
                        wait_bank_read(dve, "up", up_group(("v", j), half), 0)
                if j >= 1:
                    dve.wait_ge(u_ready, j)
                src = 0
                for i in range(j + 1):
                    dst = 1 + (i + 0) % 2
                    shift = 1 << i
                    nc.vector.tensor_tensor(row[dst], scratch[:, src, PAD:PAD + T],
                                            scratch[:, src, PAD - shift:PAD + T - shift],
                                            ALU.add).then_inc(window_added, 1)
                    added += 1
                    dve.wait_ge(window_added, added)
                    src = dst
                total, v = row[src], row[0]
                nc.vector.tensor_tensor(head[:, 0:w - 1], total[:, 0:w - 1], counts[:, 0:w - 1],
                                        ALU.mult).then_inc(head_ready, 1)
                dve.wait_ge(head_ready, 2 * j + 1)
                nc.vector.tensor_tensor(total[:, 0:w - 1], head[:, 0:w - 1], v[:, 0:w - 1],
                                        ALU.subtract).then_inc(head_ready, 1)
                dve.wait_ge(head_ready, 2 * j + 2)
                nc.vector.scalar_tensor_tensor(total[:, w - 1:T], total[:, w - 1:T], 1.0 / w, v[:, w - 1:T],
                                               ALU.mult, ALU.subtract).then_inc(pooled, 1)
                if j >= 1:
                    split_mix_lo([("v", 3), ("h", 0), ("pw", 0)][j - 1])
                split_mix_lo(("out", KC + j))
                dve.wait_ge(u_hi_ready, j + 1)
                nc.vector.tensor_tensor(act_lo[:, j, :], total, act_hi[:, j, :].bitcast(F32),
                                        ALU.subtract).then_inc(u_ready, 1)

            dve.wait_ge(cols_ready, 1)
            for j in range(KC):
                if j == 0:
                    split_mix_lo(("c", 0))
                    for i in range(8):
                        g, part = G_PW + i, slice((i % 2) * HALF, (i % 2 + 1) * HALF)
                        dve.wait_ge(act_hi_ready, i + 1)
                        nc.vector.scalar_tensor_tensor(act_lo[:, i // 2, part], psum[down_bank(g)][:, :],
                                                       cols[:, 12 + i // 2:13 + i // 2],
                                                       act_hi[:, i // 2, part].bitcast(F32),
                                                       ALU.mult, ALU.subtract).then_inc(act_ready, 1)
                        dve.wait_ge(act_ready, i + 1)
                        nc.vector.memset(head[:, 0:1], 0.0).then_inc(bank_read[down_bank(g)], 1)
                split_mix_lo(("b", j))
                for half in range(2):
                    part = slice(half * HALF, (half + 1) * HALF)
                    s_h, s = up_group(("h", j), half), up_group(("c", j), half)
                    wait_bank_read(dve, "up", s_h, 0)
                    if half == 0 and j >= 1:
                        dve.wait_ge(tap_done, 6 * j)
                    wait_group(dve, "up", s, 0)
                    nc.vector.tensor_tensor(row[1][:, part], psum[up_bank(s)][:, :], row[0][:, part],
                                            ALU.mult).then_inc(bank_read[up_bank(s)], 1)
                if j == 0:
                    for i in range(16):
                        add_group(G_POOL, i, first=True)
                if j < 3:
                    split_mix_lo(("h", j + 1))
                    if j >= 1:
                        split_mix_lo(("out", 2 * j - 1))
                else:
                    split_lo(CHUNK_LOADS[0], load_number(0, 0))
                for half in range(2):
                    part = slice(half * HALF, (half + 1) * HALF)
                    wait_bank_read(dve, "up", up_group(("c", j), half), 0)
                    for tap in range(TAPS):
                        lag = TAPS - 1 - tap
                        z = scratch[:, 1, PAD + half * HALF - lag:PAD + (half + 1) * HALF - lag]
                        weight = cols[:, 4 * tap + j:4 * tap + j + 1]
                        if tap == 0:
                            nc.vector.tensor_scalar(row[0][:, part], z, weight, None,
                                                    ALU.mult).then_inc(tap_done, 1)
                        else:
                            nc.vector.scalar_tensor_tensor(row[0][:, part], z, weight, row[0][:, part],
                                                           ALU.mult, ALU.add).then_inc(tap_done, 1)
                        dve.wait_ge(tap_done, 6 * j + 3 * half + tap + 1)
                for half in range(2):
                    part = slice(half * HALF, (half + 1) * HALF)
                    s = up_group(("b", j), half)
                    wait_group(dve, "up", s, 0)
                    nc.vector.tensor_tensor(row[0][:, part], psum[up_bank(s)][:, :], row[0][:, part],
                                            ALU.mult).then_inc(y_ready, 1)
                    dve.wait_ge(y_ready, 2 * j + half + 1)
                    nc.vector.memset(head[:, 1:2], 0.0).then_inc(bank_read[up_bank(s)], 1)
                    dve.wait_ge(act_hi_ready, 8 + 2 * j + half + 1)
                    nc.vector.tensor_tensor(act_lo[:, j, part], row[0][:, part],
                                            act_hi[:, j, part].bitcast(F32),
                                            ALU.subtract).then_inc(act_ready, 1)
                if j < 3:
                    split_mix_lo(("c", j + 1))
                    if j < 2:
                        split_mix_lo(("out", 2 * j))

            for m in range(TILES):
                add_group(G_CONV, 2 * m)
                add_group(G_CONV, 2 * m + 1)
                normalise(1, m)
                if m == 0:
                    split_lo(CHUNK_LOADS[1], load_number(0, 1))
                if m >= 2:
                    transpose_lo(1, m - 2)

            def square(order, c, i):
                k, half = order[i]
                part = slice(half * HALF, (half + 1) * HALF)
                side = slice((i % 2) * HALF, (i % 2 + 1) * HALF)
                wait_bank_read(dve, "up", S_MLP + i, 8, c)
                if not (isinstance(c, int) and c == 0 and i < 2):
                    dve.wait_ge(act_ready, A_MLP - 1 + i + 8 * c)
                nc.vector.tensor_tensor(row[1][:, side], row[0][:, side], row[0][:, side],
                                        ALU.mult).then_inc(squared_relu, 1)
                dve.wait_ge(squared_relu, i + 1 + 8 * c)
                dve.wait_ge(act_hi_ready, A_MLP + i + 1 + 8 * c)
                nc.vector.tensor_tensor(act_lo[:, k, part], row[1][:, side], act_hi[:, k, part].bitcast(F32),
                                        ALU.subtract).then_inc(act_ready, 1)

            def split_chunk_lo(what, c):
                split_lo(what, load_number(0, CHUNK_LOADS.index(what)), N_CHUNK_LOADS, c)

            transpose_lo(1, TILES - 2)
            transpose_lo(1, TILES - 1)
            square(ORDER_FIRST, 0, 0)
            split_chunk_lo(("ff2", 0), 0)
            square(ORDER_FIRST, 0, 1)
            square(ORDER_FIRST, 0, 2)
            split_chunk_lo(("ff1", 2), 0)
            square(ORDER_FIRST, 0, 3)
            split_chunk_lo(("ff2", 1), 0)
            split_chunk_lo(("ff1", 3), 0)
            square(ORDER_FIRST, 0, 4)
            split_chunk_lo(("ff2", 2), 0)
            split_chunk_lo(("ff2", 3), 0)
            for i in range(5, 8):
                square(ORDER_FIRST, 0, i)

            def down(c):
                for i in range(16):
                    add_group(G_MLP, i, c)
                    if i in (2, 4):
                        j = i // 2 - 1
                        split_lo(("ff1", j), load_number(1, j), N_CHUNK_LOADS, c)

            def chunk(c):
                for j in range(KC):
                    if j in (1, 2):
                        split_chunk_lo(("ff1", j + 1), c)
                    split_chunk_lo(("ff2", j), c)
                    square(ORDER_LATER, c, 2 * j)
                    square(ORDER_LATER, c, 2 * j + 1)

            down(0)
            with dve.Fori(1, CHUNKS - 1) as c:
                chunk(c)
                down(c)
            chunk(CHUNKS - 1)
            for m in range(TILES):
                add_group(G_MLP, 2 * m, CHUNKS - 1)
                add_group(G_MLP, 2 * m + 1, CHUNKS - 1)
                normalise(2, m)

        @block.tensor
        def _(pe):
            def products(dst, stationary, moving, first, last):
                (s_hi, s_lo), (m_hi, m_lo) = stationary, moving
                nc.tensor.matmul(dst, s_hi, m_hi, start=first, stop=False)
                nc.tensor.matmul(dst, s_hi, m_lo, start=False, stop=False)
                return nc.tensor.matmul(dst, s_lo, m_hi, start=False, stop=last)

            def transpose_tile(norm, m):
                pe.wait_ge(normed, norm * TILES + m + 1)
                for q in range(2):
                    n = 2 * (norm * TILES + m) + q
                    if n >= 2:
                        pe.wait_ge(xt_ready, n - 1)
                    for k in range(4):
                        at = (4 * q + k) * P
                        last = nc.tensor.transpose(psum[6 + q][:, k * P:(k + 1) * P],
                                                   row[m % 2][:, at:at + P], ident[:, :])
                    last.then_inc(transposed, 1)

            def wait_bank_free(kind, base, step=0, c=0):
                banks = UP_BANKS if kind == "up" else DOWN_BANKS
                if base >= banks:
                    wait_bank_read(pe, kind, base - banks, step, c)

            def up_product(slot, half, bank, done):
                for k in range(DB):
                    cols_k = slice(k * P, (k + 1) * P)
                    part = slice(half * HALF, (half + 1) * HALF)
                    last = products(psum[bank][:, :],
                                    (up_hi[:, slot, cols_k], up_lo[:, slot, cols_k]),
                                    (xt_hi[:, k, part], xt_lo[:, k, part]), k == 0, k == DB - 1)
                last.then_inc(done, 1)

            def mix_up(unit, half):
                s = up_group(unit, half)
                if half == 0:
                    pe.wait_ge(w_ready, MIX_LOADS.index(unit) + 1)
                wait_bank_free("up", s)
                up_product(MIX_UNITS.index(unit) % UP_SLOTS, half, up_bank(s), up_done)

            def down_product(base, i, c, weight_load, act_base, positions):
                g, m, n = base + i, i // 2, i % 2
                wait_bank_free("down", g, 16, c)
                for k in range(KC):
                    if i == 0:
                        load0, per_chunk = weight_load(k)
                        pe.wait_ge(w_ready, load0 + 1 + per_chunk * c)
                    if i in (0, TILES):
                        pe.wait_ge(act_ready, act_base + positions[(k, i // TILES)] + 1 + 8 * c)
                    last = products(psum[down_bank(g)][:, :],
                                    (act_hi[:, k, m * P:(m + 1) * P], act_lo[:, k, m * P:(m + 1) * P]),
                                    (down_hi[:, k, n * HALF:(n + 1) * HALF],
                                     down_lo[:, k, n * HALF:(n + 1) * HALF]), k == 0, k == KC - 1)
                last.then_inc(down_done, 1)

            later = {kh: i for i, kh in enumerate(ORDER_LATER)}
            early = {kh: i for i, kh in enumerate(ORDER_FIRST)}

            pe.wait_ge(ident_ready, 1)
            for m in range(4):
                transpose_tile(0, m)

            def pair(j, half):
                if half == 0:
                    pe.wait_ge(w_ready, MIX_LOADS.index(("v", j)) + 1)
                pe.wait_ge(xt_ready, 8 * (half + 1))
                up_product(j, half, down_bank(G_PAIR + 2 * half + j), down_done)

            pair(0, 0)
            transpose_tile(0, 4)
            transpose_tile(0, 5)
            pair(1, 0)
            transpose_tile(0, 6)
            transpose_tile(0, 7)
            pair(0, 1)
            pe.wait_ge(rows_landed, 32)
            nc.tensor.transpose(psum[0][:, 0:16], rows[:, :], ident[0:16, 0:16]).then_inc(cols_transposed, 1)
            pair(1, 1)
            pe.wait_ge(cols_ready, 1)
            for unit in MIX_UNITS[2:5]:
                for half in range(2):
                    mix_up(unit, half)
            pe.wait_ge(w_ready, MIX_LOADS.index(("pw", 0)) + 1)
            slot = MIX_UNITS.index(("pw", 0)) % UP_SLOTS
            for i in range(8):
                g, j, part = G_PW + i, i // 2, slice((i % 2) * HALF, (i % 2 + 1) * HALF)
                wait_bank_free("down", g)
                pe.wait_ge(u_ready, j + 1)
                products(psum[down_bank(g)][:, :],
                         (up_hi[:, slot, j * P:(j + 1) * P], up_lo[:, slot, j * P:(j + 1) * P]),
                         (act_hi[:, j, part], act_lo[:, j, part]), True, True).then_inc(down_done, 1)
            for half in range(2):
                mix_up(("c", 0), half)
            for i in range(16):
                down_product(G_POOL, i, 0, lambda k: (MIX_LOADS.index(("out", KC + k)), 0), 0, later)
            for unit in MIX_UNITS[7:]:
                for half in range(2):
                    mix_up(unit, half)
            for m in range(TILES):
                for n in range(2):
                    down_product(G_CONV, 2 * m + n, 0, lambda k: (MIX_LOADS.index(("out", k)), 0), 8, later)
                if m >= 2:
                    transpose_tile(1, m - 2)

            def mlp_up(order, i, c):
                j, half = order[i]
                if (j, 0) == order[i]:
                    pos = CHUNK_LOADS.index(("ff1", j))
                    pe.wait_ge(w_ready, load_number(0, pos) + 1 + N_CHUNK_LOADS * c)
                wait_bank_free("up", S_MLP + i, 8, c)
                up_product((len(MIX_UNITS) + j) % UP_SLOTS, half, up_bank(i), up_done)

            def mlp_down(c, positions):
                for i in range(16):
                    down_product(G_MLP, i, c,
                                 lambda k: (load_number(0, CHUNK_LOADS.index(("ff2", k))), N_CHUNK_LOADS),
                                 A_MLP, positions)

            pe.wait_ge(xt_ready, 2 * TILES + 8)
            mlp_up(ORDER_FIRST, 0, 0)
            transpose_tile(1, TILES - 2)
            transpose_tile(1, TILES - 1)
            mlp_up(ORDER_FIRST, 1, 0)
            pe.wait_ge(xt_ready, 2 * TILES + 16)
            for i in range(2, 8):
                mlp_up(ORDER_FIRST, i, 0)
            mlp_down(0, early)
            with pe.Fori(1, CHUNKS) as c:
                for i in range(8):
                    mlp_up(ORDER_LATER, i, c)
                mlp_down(c, later)


_INS = ["x", "norm_mix_g", "w_in", "conv_w", "pool_w", "pool_scale", "w_out", "norm_mlp_g", "w_ff1", "w_ff2",
        "norm_final_g"]


def kernel(**inputs):
    import numpy as _np
    import concourse.bacc as _bacc
    from concourse import mybir as _mybir
    from concourse.bass_utils import run_bass_kernel_spmd as _run

    nc = _bacc.Bacc("TRN2", target_bir_lowering=False, num_devices=1)
    arrays, args = {}, []
    for name in _INS:
        a = _np.ascontiguousarray(inputs[name])
        arrays[f"in_{name}"] = a
        args.append(nc.dram_tensor(f"in_{name}", a.shape, _mybir.dt.from_np(a.dtype), kind="ExternalInput").ap())
    args.append(nc.dram_tensor("out_y", (1, T, D), _mybir.dt.float32, kind="ExternalOutput").ap())
    build(nc, *args)
    r = _run(nc, [arrays], core_ids=[0])
    return r.results[0]["out_y"]
```

```python
from contextlib import ExitStack

import concourse.bass as bass
from concourse import mybir

P = 128
T = 1024
D = 1024
HALF = 512
TILES = T // P
DB = D // P
KC = 4
D_FF = 4 * D
CHUNKS = D_FF // (KC * P)
CONV = 512
WINDOWS = (2, 4, 8, 16)
TAPS = 3
EPS = 1e-6
PAD = 16
STAGES = 4
UP_SLOTS = 2

MIX_UNITS = [("v", 0), ("v", 1), ("v", 2), ("v", 3), ("h", 0), ("pw", 0), ("c", 0), ("b", 0),
             ("h", 1), ("c", 1), ("b", 1), ("h", 2), ("c", 2), ("b", 2), ("h", 3), ("c", 3), ("b", 3)]
MIX_COLUMN = {"h": 0, "b": CONV, "c": 2 * CONV, "v": 3 * CONV}
MIX_LOADS = [("v", 0), ("v", 1), ("v", 2), ("out", 4), ("v", 3), ("out", 5), ("h", 0), ("out", 6),
             ("pw", 0), ("out", 7), ("c", 0), ("b", 0), ("h", 1), ("c", 1), ("out", 0),
             ("b", 1), ("h", 2), ("out", 1), ("c", 2), ("out", 2),
             ("b", 2), ("h", 3), ("out", 3), ("c", 3), ("b", 3)]
CHUNK_LOADS = [("ff1", 0), ("ff1", 1), ("ff2", 0), ("ff1", 2), ("ff2", 1), ("ff1", 3), ("ff2", 2), ("ff2", 3)]
N_MIX_LOADS = len(MIX_LOADS)
N_CHUNK_LOADS = len(CHUNK_LOADS)
assert N_CHUNK_LOADS % STAGES == 0

UP_BANKS, DOWN_BANKS = 2, 4
G_PAIR = 0
G_PW = 4
G_POOL = G_PW + 8
G_CONV = G_POOL + 16
G_MLP = G_CONV + 16
UP_ORDER = [u for u in MIX_UNITS if u not in (("v", 0), ("v", 1), ("pw", 0))]
S_MLP = 2 * len(UP_ORDER)
ORDER_FIRST = [(0, 0), (1, 0), (0, 1), (1, 1), (2, 0), (2, 1), (3, 0), (3, 1)]
ORDER_LATER = [(j, h) for j in range(KC) for h in range(2)]
LAST_OF_UNIT = {order_id: {j: max(i for i, (u, _) in enumerate(order) if u == j) for j in range(KC)}
                for order_id, order in (("first", ORDER_FIRST), ("later", ORDER_LATER))}
A_MLP = 16
N_CONV_BLOCKS = CONV // P
ROW_TAPS, ROW_SCALE, ROW_GAIN, N_ROWS = 0, 12, 16, 24
ROWS_BANK = 5
WARM_BANK = 4
WARM = (2, 0, 0, 0, 4)


def up_group(unit, half):
    return 2 * UP_ORDER.index(unit) + half


def load_number(c, pos):
    return N_MIX_LOADS + N_CHUNK_LOADS * c + pos


def build(nc, x, norm_mix_g, w_in, conv_w, pool_w, pool_scale, w_out, norm_mlp_g, w_ff1, w_ff2,
          norm_final_g, out):
    F32, F32R = mybir.dt.float32, mybir.dt.float32r
    ACT, ALU = mybir.ActivationFunctionType, mybir.AluOpType

    x_tiles = x[0].rearrange("(m p) d -> m p d", p=P)
    out_tiles = out[0].rearrange("(m p) d -> m p d", p=P)
    w_in_cols = w_in[0].rearrange("(k p) e -> p k e", p=P)
    w_ff1_cols = w_ff1[0].rearrange("(k p) e -> p k e", p=P)

    with ExitStack() as ctx:
        def sb(name, shape, dt=F32):
            return ctx.enter_context(nc.sbuf_tensor(name, shape, dt))

        def sem(name):
            return ctx.enter_context(nc.semaphore(name))

        stream = sb("stream", [P, TILES, D])
        xt_hi = sb("xt_hi", [P, DB, T], F32R)
        xt_lo = sb("xt_lo", [P, DB, T], F32R)
        act_hi = sb("act_hi", [P, KC, T], F32R)
        act_lo = sb("act_lo", [P, KC, T], F32R)
        down_hi = sb("down_hi", [P, KC, D], F32R)
        down_lo = sb("down_lo", [P, KC, D], F32R)
        up_hi = sb("up_hi", [P, UP_SLOTS, D], F32R)
        up_lo = sb("up_lo", [P, UP_SLOTS, D], F32R)
        raw = sb("raw", [P, STAGES, D])
        scratch = sb("scratch", [P, 3, PAD + T])
        ident = sb("ident", [P, P])
        counts = sb("counts", [P, WINDOWS[-1]])
        head = sb("head", [P, WINDOWS[-1]])
        rows = sb("rows", [N_ROWS, P])
        cols = sb("cols", [P, N_ROWS])
        ones = sb("ones", [P, P])
        warm = sb("warm", [P, HALF])
        rstd_row = sb("rstd_row", [P, T])
        sumsq = sb("sumsq", [P, 2, 3 * TILES])
        half_mean = sb("half_mean", [P, 3 * TILES])
        meansq = sb("meansq", [P, 3 * TILES])
        root = sb("root", [P, 3 * TILES])
        guess = sb("guess", [P, 3 * TILES])
        newton = sb("newton", [P, 2, 3 * TILES])
        rstd = sb("rstd", [P, 3 * TILES])
        psum = [ctx.enter_context(nc.psum_tensor(f"bank{b}", [P, HALF], F32)) for b in range(8)]

        row = [scratch[:, i, PAD:PAD + T] for i in range(3)]
        gain = row[2]
        diagonal = row[2].rearrange("p (m t) -> p m t", t=P)

        x_landed = [sem(f"x_landed{m}") for m in range(TILES)]
        raw_landed = [sem(f"raw_landed{s}") for s in range(STAGES)]
        gain_landed, rows_landed, stored = sem("gain_landed"), sem("rows_landed"), sem("stored")
        ident_zeroed, ident_ready, consts_ready = sem("ident_zeroed"), sem("ident_ready"), sem("consts_ready")
        cols_transposed, cols_ready = sem("cols_transposed"), sem("cols_ready")
        ones_ready, w_gained = sem("ones_ready"), sem("w_gained")
        diagonal_ready, rstd_spread, rstd_row_ready = sem("diagonal_ready"), sem("rstd_spread"), sem("rstd_row_ready")
        squared, mean_ready, root_ready = sem("squared"), sem("mean_ready"), sem("root_ready")
        table_loaded = sem("table_loaded")
        squared_late = sem("squared_late")
        half_mean_ready, h_ready = sem("half_mean_ready"), sem("h_ready")
        newton_step, rstd_ready, normed = sem("newton_step"), sem("rstd_ready"), sem("normed")
        transposed, xt_hi_ready, xt_ready = sem("transposed"), sem("xt_hi_ready"), sem("xt_ready")
        w_hi_ready, w_ready = sem("w_hi_ready"), sem("w_ready")
        up_done, down_done = sem("up_done"), sem("down_done")
        bank_read = [sem(f"bank_read{b}") for b in range(UP_BANKS + DOWN_BANKS)]
        window_added, head_ready, pooled = sem("window_added"), sem("head_ready"), sem("pooled")
        u_hi_ready, u_ready = sem("u_hi_ready"), sem("u_ready")
        tap_done, y_ready = sem("tap_done"), sem("y_ready")
        squared_relu = sem("squared_relu")
        act_hi_ready, act_ready = sem("act_hi_ready"), sem("act_ready")

        def up_bank(s):
            return s % UP_BANKS

        def down_bank(g):
            return UP_BANKS + g % DOWN_BANKS

        def transpose_bank(norm, m, q):
            return (6, 7, 0, 1)[(2 * m + q) % 4] if norm == 0 else 6 + q

        def wait_group(eng, kind, base, step, c=0):
            eng.wait_ge(up_done if kind == "up" else down_done, base + 1 + step * c)

        def wait_bank_read(eng, kind, base, step, c=0):
            if kind == "up":
                i = base // UP_BANKS
                unit = UP_ORDER[i] if base < S_MLP else None
                gates = sum(u[0] == "b" for u in UP_ORDER[:i])
                if unit and unit[0] == "b":
                    eng.wait_ge(y_ready, 2 * unit[1] + base % 2 + 1)
                else:
                    eng.wait_ge(bank_read[up_bank(base)], i - gates + 1 + step // UP_BANKS * c)
            elif G_PW <= base < G_POOL:
                eng.wait_ge(act_ready, base - G_PW + 1)
            else:
                maps = 2 if base >= G_POOL else 0
                eng.wait_ge(bank_read[down_bank(base)], base // DOWN_BANKS - maps + 1 + step // DOWN_BANKS * c)

        def wait_unit(eng, unit):
            if unit == ("pw", 0):
                wait_group(eng, "down", G_PW + 7, 0)
            elif unit in UP_ORDER:
                wait_group(eng, "up", up_group(unit, 1), 0)
            else:
                wait_group(eng, "down", G_PAIR + 2 + unit[1], 0)

        def split_target(what, c, u=None):
            kind, j = what
            if kind in ("out", "ff2"):
                return down_hi[:, j % KC, :], down_lo[:, j % KC, :], D
            if kind == "ff1":
                slot = (len(MIX_UNITS) + j) % UP_SLOTS
            else:
                slot = MIX_UNITS.index(what) % UP_SLOTS
            width = KC * P if kind == "pw" else D
            return up_hi[:, slot, 0:width], up_lo[:, slot, 0:width], width

        block = ctx.enter_context(nc.Block())

        @block.sync
        def _(sp):
            def load(n0, per_chunk, what, c):
                kind, j = what
                slot = n0 % STAGES
                if n0 >= STAGES:
                    sp.wait_ge(w_ready, n0 - STAGES + 1 + per_chunk * c)
                dst = raw[:, slot, :]
                if kind == "out":
                    src = w_out[0, j * P:(j + 1) * P, :]
                elif kind == "ff2":
                    src = w_ff2[0, bass.ds(c * (KC * P) + j * P, P), :]
                elif kind == "ff1":
                    dst = dst.rearrange("p (k e) -> p k e", e=P)
                    src = w_ff1_cols[:, :, bass.ds(c * (KC * P) + j * P, P)]
                elif kind == "pw":
                    dst = dst[:, 0:KC * P].rearrange("p (g e) -> p g e", e=P)
                    src = pool_w[0].rearrange("g c e -> c g e")
                else:
                    e0 = MIX_COLUMN[kind] + j * P
                    dst = dst.rearrange("p (k e) -> p k e", e=P)
                    src = w_in_cols[:, :, e0:e0 + P]
                sp.dma_start(dst, src).then_inc(raw_landed[slot], 16)

            def load_gain(g):
                sp.dma_start(gain, g.partition_broadcast(P)).then_inc(gain_landed, 16)

            def load_tile(m):
                sp.dma_start(stream[:, m, :], x_tiles[m]).then_inc(x_landed[m], 16)

            load_tile(0)
            load(0, 0, MIX_LOADS[0], 0)
            for m in range(1, 5):
                load_tile(m)
            load(1, 0, MIX_LOADS[1], 0)
            for m in range(5, TILES):
                load_tile(m)
            for n in range(2, N_MIX_LOADS):
                load(n, 0, MIX_LOADS[n], 0)
                if MIX_LOADS[n] == ("c", 1):
                    sp.wait_ge(u_ready, KC)
                    load_gain(norm_mlp_g[0])
            for pos in range(N_CHUNK_LOADS):
                load(load_number(0, pos), 0, CHUNK_LOADS[pos], 0)
            sp.wait_ge(normed, TILES)
            load_gain(norm_final_g)
            with sp.Fori(1, CHUNKS) as c:
                for pos in range(N_CHUNK_LOADS):
                    load(load_number(0, pos), N_CHUNK_LOADS, CHUNK_LOADS[pos], c)
            for m in range(TILES - 1):
                sp.wait_ge(normed, TILES + 2 * m + 2)
                sp.dma_start(out_tiles[m], stream[:, m, :]).then_inc(stored, 16)
            for half in range(2):
                part = slice(half * HALF, (half + 1) * HALF)
                sp.wait_ge(normed, TILES + 2 * (TILES - 1) + half + 1)
                sp.dma_start(out_tiles[TILES - 1, :, part], stream[:, TILES - 1, part]).then_inc(stored, 16)
            sp.wait_ge(stored, 16 * (TILES + 1))

        @block.gpsimd
        def _(pool):
            nc.gpsimd.memset(ones[:, :], 1.0).then_inc(ones_ready, 1)
            nc.gpsimd.memset(warm[:, :], 0.0).then_inc(ones_ready, 1)
            nc.gpsimd.memset(ident[:, :], 0.0).then_inc(ident_zeroed, 1)
            pool.wait_ge(ident_zeroed, 1)
            nc.gpsimd.affine_select(out=ident[:, :], in_=ident[:, :], compare_op=ALU.not_equal, fill=1.0,
                                    base=0, pattern=[[-1, P]], channel_multiplier=1).then_inc(ident_ready, 1)
            nc.gpsimd.memset(scratch[:, :, 0:PAD], 0.0).then_inc(consts_ready, 1)
            for t in range(WINDOWS[-1]):
                nc.gpsimd.memset(counts[:, t:t + 1], 1.0 / (t + 1)).then_inc(consts_ready, 1)
            pool.wait_ge(cols_ready, 1)
            for n, (kind, _) in enumerate(MIX_LOADS):
                if kind in MIX_COLUMN:
                    pool.wait_ge(raw_landed[n % STAGES], 16 * (n // STAGES + 1))
                    block_k = raw[:, n % STAGES, :].rearrange("p (k e) -> p k e", e=P)
                    nc.gpsimd.tensor_tensor(block_k, block_k,
                                            cols[:, ROW_GAIN:ROW_GAIN + DB].unsqueeze(2).to_broadcast([P, DB, P]),
                                            ALU.mult).then_inc(w_gained, 1)

        N_CONSTS = 1 + WINDOWS[-1]

        @block.scalar
        def _(act):
            def split_hi(what, n0, per_chunk=0, c=0):
                hi, _, width = split_target(what, c)
                if what[0] in MIX_COLUMN:
                    act.wait_ge(w_gained, sum(kind in MIX_COLUMN for kind, _ in MIX_LOADS[:n0]) + 1)
                else:
                    act.wait_ge(raw_landed[n0 % STAGES], 16 * (n0 // STAGES + 1) + 16 * (per_chunk // STAGES) * c)
                nc.scalar.activation(hi, raw[:, n0 % STAGES, 0:width], ACT.Copy).then_inc(w_hi_ready, 1)

            def split_mix_hi(what):
                n = MIX_LOADS.index(what)
                if what[0] != "out":
                    u = MIX_UNITS.index(what)
                    if u >= UP_SLOTS:
                        wait_unit(act, MIX_UNITS[u - UP_SLOTS])
                elif what[1] < KC:
                    wait_group(act, "down", G_CONV - 1, 0)
                split_hi(what, n)

            def root_of_mean(q, at):
                act.wait_ge(mean_ready, q + 1)
                nc.scalar.activation(root[:, at], meansq[:, at], ACT.Sqrt).then_inc(root_ready, 1)

            def root_mean_square(norm, m):
                i = norm * TILES + m
                base = G_CONV if norm == 1 else G_MLP + 16 * (CHUNKS - 1)
                for half in range(2):
                    part = slice(half * HALF, (half + 1) * HALF)
                    wait_bank_read(act, "down", base + 2 * m + half, 0)
                    if norm == 1 and m >= 2:
                        act.wait_ge(transposed, 2 * TILES + 2 * (m - 1))
                    nc.scalar.activation(row[m % 2][:, part], stream[:, m, part], ACT.Square,
                                         accum_out=sumsq[:, half, i:i + 1]).then_inc(squared, 1)
                root_of_mean(i - TILES + 1, slice(i, i + 1))

            def transpose_hi(norm, m):
                for q in range(2):
                    n = 2 * (norm * TILES + m) + q
                    act.wait_ge(transposed, n + 1)
                    nc.scalar.activation(xt_hi[:, 4 * q:4 * q + 4, m * P:(m + 1) * P],
                                         psum[transpose_bank(norm, m, q)][:, :].rearrange(
                                             "p (k t) -> p k t", t=P),
                                         ACT.Copy).then_inc(xt_hi_ready, 1)

            def sum_of_squares(m):
                act.wait_ge(x_landed[m], 16)
                if m >= 2:
                    act.wait_ge(squared, m - 1)
                nc.scalar.activation(row[m % 2], stream[:, m, :], ACT.Square,
                                     accum_out=sumsq[:, 0, m:m + 1]).then_inc(squared, 1)

            act.wait_ge(ones_ready, 1)
            nc.scalar.activation(root[:, 0:1], ones[:, 0:1], ACT.Sqrt).then_inc(table_loaded, 1)

            act.dma_start(rows[ROW_GAIN:ROW_GAIN + DB, :],
                          norm_mix_g[0].rearrange("(k p) -> k p", p=P)).then_inc(rows_landed, 16)
            act.dma_start(rows[ROW_TAPS:ROW_TAPS + 12, :],
                          conv_w[0].rearrange("t (j p) -> (t j) p", p=P)).then_inc(rows_landed, 16)
            act.dma_start(rows[ROW_SCALE:ROW_SCALE + 4, :],
                          pool_scale[0].rearrange("(j p) -> j p", p=P)).then_inc(rows_landed, 16)
            transpose_hi(0, 0)
            act.wait_ge(cols_transposed, 1)
            nc.scalar.activation(cols[:, :], psum[ROWS_BANK][:, 0:N_ROWS], ACT.Copy).then_inc(cols_ready, 1)
            transpose_hi(0, 1)
            split_mix_hi(("v", 0))
            transpose_hi(0, 2)
            transpose_hi(0, 3)
            for m in range(4):
                sum_of_squares(m)
            transpose_hi(0, 4)
            split_mix_hi(("v", 1))
            act.wait_ge(table_loaded, 1)
            root_of_mean(0, slice(0, TILES))
            for m in range(5, TILES):
                transpose_hi(0, m)
            for half in range(2):
                act.wait_ge(rstd_spread, half + 1)
                nc.scalar.activation(rstd_row[:, half * HALF:(half + 1) * HALF], psum[6 + half][:, :],
                                     ACT.Copy).then_inc(rstd_row_ready, 1)

            split_mix_hi(("v", 2))
            for j in range(KC):
                if j >= 1:
                    split_mix_hi([("v", 3), ("h", 0), ("pw", 0)][j - 1])
                split_mix_hi(("out", KC + j))
                act.wait_ge(pooled, j + 1)
                nc.scalar.activation(act_hi[:, j, :], row[1 + j % 2], ACT.Copy).then_inc(u_hi_ready, 1)

            for j in range(N_CONV_BLOCKS):
                if j == 0:
                    split_mix_hi(("c", 0))
                    for i in range(8):
                        g = G_PW + i
                        wait_group(act, "down", g, 0)
                        nc.scalar.activation(act_hi[:, i // 2, (i % 2) * HALF:(i % 2 + 1) * HALF],
                                             psum[down_bank(g)][:, :], ACT.Copy,
                                             scale=cols[:, ROW_SCALE + i // 2:ROW_SCALE + i // 2 + 1]).then_inc(act_hi_ready, 1)
                split_mix_hi(("b", j))
                if j < 3:
                    split_mix_hi(("h", j + 1))
                    if j >= 1:
                        split_mix_hi(("out", 2 * j - 1))
                else:
                    wait_unit(act, ("c", 3))
                    split_hi(CHUNK_LOADS[0], load_number(0, 0))
                for half in range(2):
                    act.wait_ge(y_ready, 2 * j + half + 1)
                    nc.scalar.activation(act_hi[:, j, half * HALF:(half + 1) * HALF],
                                         row[0][:, half * HALF:(half + 1) * HALF],
                                         ACT.Copy).then_inc(act_hi_ready, 1)
                if j < 3:
                    split_mix_hi(("c", j + 1))
                    if j < 2:
                        split_mix_hi(("out", 2 * j))
                else:
                    wait_unit(act, ("b", 3))
                    split_hi(CHUNK_LOADS[1], load_number(0, 1))

            for m in range(TILES):
                root_mean_square(1, m)
                if m >= 2:
                    transpose_hi(1, m - 2)

            def relu(order, c, i):
                k, half = order[i]
                act.wait_ge(squared_relu, i - 1 + 8 * c) if not (isinstance(c, int) and c == 0 and i < 2) else None
                wait_group(act, "up", S_MLP + i, 8, c)
                r = row[0][:, (i % 2) * HALF:(i % 2 + 1) * HALF]
                nc.scalar.activation(r, psum[up_bank(i)][:, :], ACT.Relu).then_inc(bank_read[up_bank(i)], 1)
                wait_bank_read(act, "up", S_MLP + i, 8, c)
                nc.scalar.activation(act_hi[:, k, half * HALF:(half + 1) * HALF], r,
                                     ACT.Square).then_inc(act_hi_ready, 1)

            def split_ff1(j, c, order_id):
                wait_group(act, "up", S_MLP + LAST_OF_UNIT[order_id][j - 2], 8, c)
                pos = CHUNK_LOADS.index(("ff1", j))
                split_hi(("ff1", j), load_number(0, pos), N_CHUNK_LOADS, c)

            def split_ff2(k, c):
                pos = CHUNK_LOADS.index(("ff2", k))
                split_hi(("ff2", k), load_number(0, pos), N_CHUNK_LOADS, c)

            def split_next_ff1(c):
                for j in range(2):
                    wait_group(act, "up", S_MLP + LAST_OF_UNIT["later"][2 + j], 8, c)
                    split_hi(("ff1", j), load_number(1, j), N_CHUNK_LOADS, c)

            transpose_hi(1, TILES - 2)
            transpose_hi(1, TILES - 1)
            wait_group(act, "down", G_MLP - 1, 0)
            relu(ORDER_FIRST, 0, 0)
            split_ff2(0, 0)
            relu(ORDER_FIRST, 0, 1)
            relu(ORDER_FIRST, 0, 2)
            split_ff1(2, 0, "first")
            relu(ORDER_FIRST, 0, 3)
            split_ff2(1, 0)
            split_ff1(3, 0, "first")
            relu(ORDER_FIRST, 0, 4)
            split_ff2(2, 0)
            split_ff2(3, 0)
            for i in range(5, 8):
                relu(ORDER_FIRST, 0, i)
            split_next_ff1(0)

            def chunk(c):
                wait_group(act, "down", G_MLP - 1, 16, c)
                for j in range(KC):
                    if j in (1, 2):
                        split_ff1(j + 1, c, "later")
                    if j == 0:
                        split_ff2(0, c)
                    elif j < 3:
                        split_ff2(j, c)
                    else:
                        split_ff2(3, c)
                    relu(ORDER_LATER, c, 2 * j)
                    relu(ORDER_LATER, c, 2 * j + 1)

            with act.Fori(1, CHUNKS - 1) as c:
                chunk(c)
                split_next_ff1(c)
            chunk(CHUNKS - 1)
            for m in range(TILES):
                root_mean_square(2, m)

        @block.vector
        def _(dve):
            def split_lo(what, n0, per_chunk=0, c=0):
                hi, lo, width = split_target(what, c)
                dve.wait_ge(w_hi_ready, n0 + 1 + per_chunk * c)
                nc.vector.tensor_tensor(lo, raw[:, n0 % STAGES, 0:width], hi.bitcast(F32),
                                        ALU.subtract).then_inc(w_ready, 1)

            def split_mix_lo(what):
                split_lo(what, MIX_LOADS.index(what))

            def reciprocal_root(q, at):
                dve.wait_ge(root_ready, q + 1)
                nc.vector.reciprocal(guess[:, at], root[:, at]).then_inc(newton_step, 1)
                dve.wait_ge(newton_step, 4 * q + 1)
                nc.vector.tensor_tensor(newton[:, 0, at], guess[:, at], guess[:, at],
                                        ALU.mult).then_inc(newton_step, 1)
                dve.wait_ge(newton_step, 4 * q + 2)
                nc.vector.scalar_tensor_tensor(newton[:, 1, at], newton[:, 0, at], -0.5, meansq[:, at],
                                               ALU.mult, ALU.mult).then_inc(newton_step, 1)
                dve.wait_ge(newton_step, 4 * q + 3)
                nc.vector.tensor_scalar(newton[:, 0, at], newton[:, 1, at], 1.5, None,
                                        ALU.add).then_inc(newton_step, 1)
                dve.wait_ge(newton_step, 4 * q + 4)
                nc.vector.tensor_tensor(rstd[:, at], guess[:, at], newton[:, 0, at],
                                        ALU.mult).then_inc(rstd_ready, 1)
                dve.wait_ge(rstd_ready, q + 1)

            def normalise(norm, m):
                i = norm * TILES + m
                q = i - TILES + 1
                at = slice(i, i + 1)
                dve.wait_ge(squared, TILES // 2 + 2 * (q - 1) + 1)
                nc.vector.tensor_scalar(half_mean[:, at], sumsq[:, 0, at], 1.0 / D, EPS, ALU.mult,
                                        ALU.add).then_inc(half_mean_ready, 1)
                dve.wait_ge(half_mean_ready, q)
                dve.wait_ge(squared, TILES // 2 + 2 * (q - 1) + 2)
                nc.vector.scalar_tensor_tensor(meansq[:, at], sumsq[:, 1, at], 1.0 / D, half_mean[:, at],
                                               ALU.mult, ALU.add).then_inc(mean_ready, 1)
                reciprocal_root(q, at)
                if m == 0:
                    dve.wait_ge(gain_landed, 16 * norm)
                if norm == 1:
                    nc.vector.scalar_tensor_tensor(row[m % 2], stream[:, m, :], rstd[:, at], gain,
                                                   ALU.mult, ALU.mult).then_inc(normed, 1)
                else:
                    for half in range(2):
                        part = slice(half * HALF, (half + 1) * HALF)
                        nc.vector.scalar_tensor_tensor(stream[:, m, part], stream[:, m, part], rstd[:, at],
                                                       gain[:, part], ALU.mult, ALU.mult).then_inc(normed, 1)

            def transpose_lo(norm, m):
                for q in range(2):
                    n = 2 * (norm * TILES + m) + q
                    hi = xt_hi[:, 4 * q:4 * q + 4, m * P:(m + 1) * P]
                    dve.wait_ge(xt_hi_ready, n + 1)
                    nc.vector.tensor_tensor(xt_lo[:, 4 * q:4 * q + 4, m * P:(m + 1) * P],
                                            psum[transpose_bank(norm, m, q)][:, :].rearrange(
                                                "p (k t) -> p k t", t=P),
                                            hi.bitcast(F32), ALU.subtract).then_inc(xt_ready, 1)

            def add_group(base, i, c=0, first=False):
                g = base + i
                dst = stream[:, i // 2, (i % 2) * HALF:(i % 2 + 1) * HALF]
                if not first:
                    wait_bank_read(dve, "down", g - 16, 16, c)
                wait_group(dve, "down", g, 16, c)
                nc.vector.tensor_tensor(dst, psum[down_bank(g)][:, :], dst,
                                        ALU.add).then_inc(bank_read[down_bank(g)], 1)

            transpose_lo(0, 0)
            transpose_lo(0, 1)
            transpose_lo(0, 2)
            split_mix_lo(("v", 0))
            transpose_lo(0, 3)
            for m in range(4, TILES):
                dve.wait_ge(x_landed[m], 16)
                if m >= 5:
                    dve.wait_ge(squared_late, m - 4)
                nc.vector.tensor_tensor_reduce(out=row[2], in0=stream[:, m, :], in1=stream[:, m, :],
                                               scale=1.0, scalar=0.0, op0=ALU.mult, op1=ALU.add,
                                               accum_out=sumsq[:, 0, m:m + 1]).then_inc(squared_late, 1)
                if m == 5:
                    transpose_lo(0, 4)
                    split_mix_lo(("v", 1))
            dve.wait_ge(squared, 4)
            dve.wait_ge(squared_late, 4)
            nc.vector.tensor_scalar(meansq[:, 0:TILES], sumsq[:, 0, 0:TILES], 1.0 / D, EPS, ALU.mult,
                                    ALU.add).then_inc(mean_ready, 1)
            reciprocal_root(0, slice(0, TILES))
            dve.wait_ge(ident_ready, 1)
            for m in range(TILES):
                nc.vector.tensor_scalar(diagonal[:, m, :], ident[:, :], rstd[:, m:m + 1], None,
                                        ALU.mult).then_inc(diagonal_ready, 1)

            for m in range(5, TILES):
                transpose_lo(0, m)

            def from_psum(row_part, psum_part, rstd_part, done):
                nc.vector.tensor_tensor(row_part, psum_part, rstd_part, ALU.mult).then_inc(done, 1)

            split_mix_lo(("v", 2))
            dve.wait_ge(consts_ready, N_CONSTS)
            dve.wait_ge(rstd_row_ready, 2)
            added = 0
            for j in range(KC):
                w = WINDOWS[j]
                for half in range(2):
                    part = slice(half * HALF, (half + 1) * HALF)
                    kind, g = ("down", G_PAIR + 2 * half + j) if j < 2 else ("up", up_group(("v", j), half))
                    bank = down_bank(g) if j < 2 else up_bank(g)
                    wait_group(dve, kind, g, 0)
                    if j >= 1:
                        dve.wait_ge(pooled, j)
                    from_psum(row[0][:, part], psum[bank][:, :], rstd_row[:, part], bank_read[bank])
                for half in range(2):
                    if j < 2:
                        wait_bank_read(dve, "down", G_PAIR + 2 * half + j, 0)
                    else:
                        wait_bank_read(dve, "up", up_group(("v", j), half), 0)
                if j >= 1:
                    dve.wait_ge(u_ready, j)
                src = 0
                for i in range(j + 1):
                    dst = 1 + i % 2
                    shift = 1 << i
                    nc.vector.tensor_tensor(row[dst], scratch[:, src, PAD:PAD + T],
                                            scratch[:, src, PAD - shift:PAD + T - shift],
                                            ALU.add).then_inc(window_added, 1)
                    added += 1
                    dve.wait_ge(window_added, added)
                    src = dst
                total, v = row[src], row[0]
                nc.vector.tensor_tensor(head[:, 0:w - 1], total[:, 0:w - 1], counts[:, 0:w - 1],
                                        ALU.mult).then_inc(head_ready, 1)
                dve.wait_ge(head_ready, 2 * j + 1)
                nc.vector.tensor_tensor(total[:, 0:w - 1], head[:, 0:w - 1], v[:, 0:w - 1],
                                        ALU.subtract).then_inc(head_ready, 1)
                dve.wait_ge(head_ready, 2 * j + 2)
                nc.vector.scalar_tensor_tensor(total[:, w - 1:T], total[:, w - 1:T], 1.0 / w, v[:, w - 1:T],
                                               ALU.mult, ALU.subtract).then_inc(pooled, 1)
                if j >= 1:
                    split_mix_lo([("v", 3), ("h", 0), ("pw", 0)][j - 1])
                split_mix_lo(("out", KC + j))
                dve.wait_ge(u_hi_ready, j + 1)
                nc.vector.tensor_tensor(act_lo[:, j, :], total, act_hi[:, j, :].bitcast(F32),
                                        ALU.subtract).then_inc(u_ready, 1)

            dve.wait_ge(cols_ready, 1)
            for j in range(N_CONV_BLOCKS):
                for half in range(2):
                    part = slice(half * HALF, (half + 1) * HALF)
                    s = up_group(("h", j), half)
                    if j == 0:
                        dve.wait_ge(pooled, KC)
                    else:
                        dve.wait_ge(act_ready, 8 + 2 * j)
                    wait_group(dve, "up", s, 0)
                    from_psum(row[0][:, part], psum[up_bank(s)][:, :], rstd_row[:, part],
                              bank_read[up_bank(s)])
                for half in range(2):
                    part = slice(half * HALF, (half + 1) * HALF)
                    wait_bank_read(dve, "up", up_group(("h", j), half), 0)
                    nc.vector.tensor_tensor(row[0][:, part], row[0][:, part], rstd_row[:, part],
                                            ALU.mult).then_inc(h_ready, 1)
                if j == 0:
                    split_mix_lo(("c", 0))
                    for i in range(8):
                        g, part = G_PW + i, slice((i % 2) * HALF, (i % 2 + 1) * HALF)
                        dve.wait_ge(act_hi_ready, i + 1)
                        nc.vector.scalar_tensor_tensor(act_lo[:, i // 2, part], psum[down_bank(g)][:, :],
                                                       cols[:, ROW_SCALE + i // 2:ROW_SCALE + i // 2 + 1],
                                                       act_hi[:, i // 2, part].bitcast(F32),
                                                       ALU.mult, ALU.subtract).then_inc(act_ready, 1)
                split_mix_lo(("b", j))
                for half in range(2):
                    part = slice(half * HALF, (half + 1) * HALF)
                    s = up_group(("c", j), half)
                    dve.wait_ge(h_ready, 2 * j + half + 1)
                    if half == 0 and j >= 1:
                        dve.wait_ge(tap_done, 8 * j)
                    wait_group(dve, "up", s, 0)
                    nc.vector.tensor_tensor(row[1][:, part], psum[up_bank(s)][:, :], row[0][:, part],
                                            ALU.mult).then_inc(bank_read[up_bank(s)], 1)
                if j == 0:
                    for i in range(16):
                        add_group(G_POOL, i, first=True)
                if j < 3:
                    split_mix_lo(("h", j + 1))
                    if j >= 1:
                        split_mix_lo(("out", 2 * j - 1))
                else:
                    split_lo(CHUNK_LOADS[0], load_number(0, 0))
                for half in range(2):
                    part = slice(half * HALF, (half + 1) * HALF)
                    wait_bank_read(dve, "up", up_group(("c", j), half), 0)
                    for tap in range(TAPS):
                        lag = TAPS - 1 - tap
                        z = scratch[:, 1, PAD + half * HALF - lag:PAD + (half + 1) * HALF - lag]
                        weight = cols[:, ROW_TAPS + 4 * tap + j:ROW_TAPS + 4 * tap + j + 1]
                        if tap == 0:
                            nc.vector.tensor_scalar(row[0][:, part], z, weight, None,
                                                    ALU.mult).then_inc(tap_done, 1)
                        else:
                            nc.vector.scalar_tensor_tensor(row[0][:, part], z, weight, row[0][:, part],
                                                           ALU.mult, ALU.add).then_inc(tap_done, 1)
                        dve.wait_ge(tap_done, 8 * j + 4 * half + tap + 1)
                    nc.vector.tensor_tensor(row[0][:, part], row[0][:, part], rstd_row[:, part],
                                            ALU.mult).then_inc(tap_done, 1)
                for half in range(2):
                    part = slice(half * HALF, (half + 1) * HALF)
                    s = up_group(("b", j), half)
                    dve.wait_ge(tap_done, 8 * j + 4 * half + 4)
                    wait_group(dve, "up", s, 0)
                    nc.vector.tensor_tensor(row[0][:, part], psum[up_bank(s)][:, :], row[0][:, part],
                                            ALU.mult).then_inc(y_ready, 1)
                    dve.wait_ge(y_ready, 2 * j + half + 1)
                    dve.wait_ge(act_hi_ready, 8 + 2 * j + half + 1)
                    nc.vector.tensor_tensor(act_lo[:, j, part], row[0][:, part],
                                            act_hi[:, j, part].bitcast(F32),
                                            ALU.subtract).then_inc(act_ready, 1)
                if j < 3:
                    split_mix_lo(("c", j + 1))
                    if j < 2:
                        split_mix_lo(("out", 2 * j))

            for m in range(TILES):
                add_group(G_CONV, 2 * m)
                add_group(G_CONV, 2 * m + 1)
                normalise(1, m)
                if m == 0:
                    split_lo(CHUNK_LOADS[1], load_number(0, 1))
                if m >= 2:
                    transpose_lo(1, m - 2)

            def square(order, c, i):
                k, half = order[i]
                part = slice(half * HALF, (half + 1) * HALF)
                side = slice((i % 2) * HALF, (i % 2 + 1) * HALF)
                wait_bank_read(dve, "up", S_MLP + i, 8, c)
                if not (isinstance(c, int) and c == 0 and i < 2):
                    dve.wait_ge(act_ready, A_MLP - 1 + i + 8 * c)
                nc.vector.tensor_tensor(row[1][:, side], row[0][:, side], row[0][:, side],
                                        ALU.mult).then_inc(squared_relu, 1)
                dve.wait_ge(squared_relu, i + 1 + 8 * c)
                dve.wait_ge(act_hi_ready, A_MLP + i + 1 + 8 * c)
                nc.vector.tensor_tensor(act_lo[:, k, part], row[1][:, side], act_hi[:, k, part].bitcast(F32),
                                        ALU.subtract).then_inc(act_ready, 1)

            def split_chunk_lo(what, c):
                split_lo(what, load_number(0, CHUNK_LOADS.index(what)), N_CHUNK_LOADS, c)

            transpose_lo(1, TILES - 2)
            transpose_lo(1, TILES - 1)
            square(ORDER_FIRST, 0, 0)
            split_chunk_lo(("ff2", 0), 0)
            square(ORDER_FIRST, 0, 1)
            square(ORDER_FIRST, 0, 2)
            split_chunk_lo(("ff1", 2), 0)
            square(ORDER_FIRST, 0, 3)
            split_chunk_lo(("ff2", 1), 0)
            split_chunk_lo(("ff1", 3), 0)
            square(ORDER_FIRST, 0, 4)
            split_chunk_lo(("ff2", 2), 0)
            split_chunk_lo(("ff2", 3), 0)
            for i in range(5, 8):
                square(ORDER_FIRST, 0, i)

            def down(c):
                for i in range(16):
                    add_group(G_MLP, i, c)
                    if i in (2, 4):
                        j = i // 2 - 1
                        split_lo(("ff1", j), load_number(1, j), N_CHUNK_LOADS, c)

            def chunk(c):
                for j in range(KC):
                    if j in (1, 2):
                        split_chunk_lo(("ff1", j + 1), c)
                    split_chunk_lo(("ff2", j), c)
                    square(ORDER_LATER, c, 2 * j)
                    square(ORDER_LATER, c, 2 * j + 1)

            down(0)
            with dve.Fori(1, CHUNKS - 1) as c:
                chunk(c)
                down(c)
            chunk(CHUNKS - 1)
            for m in range(TILES):
                add_group(G_MLP, 2 * m, CHUNKS - 1)
                add_group(G_MLP, 2 * m + 1, CHUNKS - 1)
                normalise(2, m)

        @block.tensor
        def _(pe):
            def products(dst, stationary, moving, first, last):
                (s_hi, s_lo), (m_hi, m_lo) = stationary, moving
                nc.tensor.matmul(dst, s_hi, m_hi, start=first, stop=False)
                nc.tensor.matmul(dst, s_hi, m_lo, start=False, stop=False)
                return nc.tensor.matmul(dst, s_lo, m_hi, start=False, stop=last)

            def transpose_tile(norm, m):
                if norm == 0:
                    pe.wait_ge(x_landed[m], 16)
                else:
                    pe.wait_ge(normed, m + 1)
                for q in range(2):
                    n = 2 * (norm * TILES + m) + q
                    reuse = 4 if norm == 0 else 2
                    if n >= reuse:
                        pe.wait_ge(xt_ready, n - reuse + 1)
                    for k in range(4):
                        at = (4 * q + k) * P
                        src = stream[:, m, at:at + P] if norm == 0 else row[m % 2][:, at:at + P]
                        last = nc.tensor.transpose(psum[transpose_bank(norm, m, q)][:, k * P:(k + 1) * P],
                                                   src, ident[:, :])
                    last.then_inc(transposed, 1)

            def wait_bank_free(kind, base, step=0, c=0):
                banks = UP_BANKS if kind == "up" else DOWN_BANKS
                if base >= banks:
                    wait_bank_read(pe, kind, base - banks, step, c)

            def up_product(slot, half, bank, done, between={}):
                for k in range(DB):
                    if k in between:
                        between[k]()
                    cols_k = slice(k * P, (k + 1) * P)
                    part = slice(half * HALF, (half + 1) * HALF)
                    last = products(psum[bank][:, :],
                                    (up_hi[:, slot, cols_k], up_lo[:, slot, cols_k]),
                                    (xt_hi[:, k, part], xt_lo[:, k, part]), k == 0, k == DB - 1)
                last.then_inc(done, 1)

            def mix_up(unit, half):
                s = up_group(unit, half)
                if half == 0:
                    pe.wait_ge(w_ready, MIX_LOADS.index(unit) + 1)
                wait_bank_free("up", s)
                up_product(MIX_UNITS.index(unit) % UP_SLOTS, half, up_bank(s), up_done)

            def down_product(base, i, c, weight_load, act_base, positions):
                g, m, n = base + i, i // 2, i % 2
                wait_bank_free("down", g, 16, c)
                for k in range(KC):
                    if i == 0:
                        load0, per_chunk = weight_load(k)
                        pe.wait_ge(w_ready, load0 + 1 + per_chunk * c)
                    if i in (0, TILES):
                        pe.wait_ge(act_ready, act_base + positions[(k, i // TILES)] + 1 + 8 * c)
                    last = products(psum[down_bank(g)][:, :],
                                    (act_hi[:, k, m * P:(m + 1) * P], act_lo[:, k, m * P:(m + 1) * P]),
                                    (down_hi[:, k, n * HALF:(n + 1) * HALF],
                                     down_lo[:, k, n * HALF:(n + 1) * HALF]), k == 0, k == KC - 1)
                last.then_inc(down_done, 1)

            later = {kh: i for i, kh in enumerate(ORDER_LATER)}
            early = {kh: i for i, kh in enumerate(ORDER_FIRST)}

            def transpose_rows():
                pe.wait_ge(rows_landed, 48)
                nc.tensor.transpose(psum[ROWS_BANK][:, 0:N_ROWS], rows[:, :],
                                    ident[0:N_ROWS, 0:N_ROWS]).then_inc(cols_transposed, 1)

            def warm_up(n):
                for _ in range(n):
                    nc.tensor.matmul(psum[WARM_BANK][:, :], ones[:, :], warm[:, :], start=True, stop=True)

            pe.wait_ge(ones_ready, 2)
            warm_up(WARM[0])
            pe.wait_ge(ident_ready, 1)

            def pair(j, half, between={}):
                if half == 0:
                    pe.wait_ge(w_ready, MIX_LOADS.index(("v", j)) + 1)
                pe.wait_ge(xt_ready, 8 * (half + 1))
                up_product(j, half, down_bank(G_PAIR + 2 * half + j), down_done, between)

            def spread_rstd():
                pe.wait_ge(ones_ready, 1)
                pe.wait_ge(xt_ready, 2 * TILES)
                pe.wait_ge(diagonal_ready, TILES)
                for m in range(TILES):
                    last = nc.tensor.matmul(psum[6 + m // 4][:, (m % 4) * P:(m % 4 + 1) * P], ones[:, :],
                                            diagonal[:, m, :], start=True, stop=True)
                    if m % 4 == 3:
                        last.then_inc(rstd_spread, 1)

            for m in range(4):
                transpose_tile(0, m)
                if m == 0:
                    transpose_rows()
                warm_up(WARM[1 + m])
            pair(0, 0, {4: lambda: transpose_tile(0, 4)})
            transpose_tile(0, 5)
            pair(1, 0, {3: lambda: transpose_tile(0, 6), 6: lambda: transpose_tile(0, 7)})
            pair(0, 1, {4: spread_rstd})
            pe.wait_ge(cols_ready, 1)
            pair(1, 1)
            for unit in MIX_UNITS[2:5]:
                for half in range(2):
                    mix_up(unit, half)

            def pooling_maps(i0):
                slot = MIX_UNITS.index(("pw", 0)) % UP_SLOTS
                for i in range(i0, i0 + 4):
                    g, j, part = G_PW + i, i // 2, slice((i % 2) * HALF, (i % 2 + 1) * HALF)
                    wait_bank_free("down", g)
                    pe.wait_ge(u_ready, j + 1)
                    products(psum[down_bank(g)][:, :],
                             (up_hi[:, slot, j * P:(j + 1) * P], up_lo[:, slot, j * P:(j + 1) * P]),
                             (act_hi[:, j, part], act_lo[:, j, part]), True, True).then_inc(down_done, 1)

            pe.wait_ge(w_ready, MIX_LOADS.index(("pw", 0)) + 1)
            pooling_maps(0)
            mix_up(("c", 0), 0)
            pooling_maps(4)
            mix_up(("c", 0), 1)
            for i in range(16):
                down_product(G_POOL, i, 0, lambda k: (MIX_LOADS.index(("out", KC + k)), 0), 0, later)
            for unit in MIX_UNITS[7:]:
                for half in range(2):
                    mix_up(unit, half)
            for m in range(TILES):
                for n in range(2):
                    down_product(G_CONV, 2 * m + n, 0, lambda k: (MIX_LOADS.index(("out", k)), 0), 8, later)
                if m >= 2:
                    transpose_tile(1, m - 2)

            def mlp_up(order, i, c, between={}):
                j, half = order[i]
                if (j, 0) == order[i]:
                    pos = CHUNK_LOADS.index(("ff1", j))
                    pe.wait_ge(w_ready, load_number(0, pos) + 1 + N_CHUNK_LOADS * c)
                wait_bank_free("up", S_MLP + i, 8, c)
                up_product((len(MIX_UNITS) + j) % UP_SLOTS, half, up_bank(i), up_done, between)

            def mlp_down(c, positions):
                for i in range(16):
                    down_product(G_MLP, i, c,
                                 lambda k: (load_number(0, CHUNK_LOADS.index(("ff2", k))), N_CHUNK_LOADS),
                                 A_MLP, positions)

            pe.wait_ge(xt_ready, 2 * TILES + 8)
            mlp_up(ORDER_FIRST, 0, 0, {4: lambda: transpose_tile(1, TILES - 2)})
            mlp_up(ORDER_FIRST, 1, 0, {1: lambda: transpose_tile(1, TILES - 1)})
            pe.wait_ge(xt_ready, 2 * TILES + 16)
            for i in range(2, 8):
                mlp_up(ORDER_FIRST, i, 0)
            mlp_down(0, early)
            with pe.Fori(1, CHUNKS) as c:
                for i in range(8):
                    mlp_up(ORDER_LATER, i, c)
                mlp_down(c, later)


_INS = ["x", "norm_mix_g", "w_in", "conv_w", "pool_w", "pool_scale", "w_out", "norm_mlp_g", "w_ff1", "w_ff2",
        "norm_final_g"]


def kernel(**inputs):
    import numpy as _np
    import concourse.bacc as _bacc
    from concourse import mybir as _mybir
    from concourse.bass_utils import run_bass_kernel_spmd as _run

    nc = _bacc.Bacc("TRN2", target_bir_lowering=False, num_devices=1,
                     dynamic_dma_scratch_size=1024)
    arrays, args = {}, []
    for name in _INS:
        a = _np.ascontiguousarray(inputs[name])
        arrays[f"in_{name}"] = a
        args.append(nc.dram_tensor(f"in_{name}", a.shape, _mybir.dt.from_np(a.dtype), kind="ExternalInput").ap())
    args.append(nc.dram_tensor("out_y", (1, T, D), _mybir.dt.float32, kind="ExternalOutput").ap())
    build(nc, *args)
    r = _run(nc, [arrays], core_ids=[0])
    return r.results[0]["out_y"]
```

```python
from contextlib import ExitStack

import concourse.bass as bass
from concourse import mybir

P = 128
T = 1024
D = 1024
HALF = 512
TILES = T // P
DB = D // P
KC = 4
D_FF = 4 * D
CHUNKS = D_FF // (KC * P)
CONV = 512
WINDOWS = (2, 4, 8, 16)
TAPS = 3
EPS = 1e-6
PAD = 16
STAGES = 4
UP_SLOTS = 2

MIX_UNITS = [("v", 0), ("v", 1), ("v", 2), ("v", 3), ("h", 0), ("pw", 0), ("c", 0), ("b", 0),
             ("h", 1), ("c", 1), ("b", 1), ("h", 2), ("c", 2), ("b", 2), ("h", 3), ("c", 3), ("b", 3)]
MIX_COLUMN = {"h": 0, "b": CONV, "c": 2 * CONV, "v": 3 * CONV}
MIX_LOADS = [("v", 0), ("v", 1), ("v", 2), ("out", 4), ("v", 3), ("out", 5), ("h", 0), ("out", 6),
             ("pw", 0), ("c", 0), ("out", 7), ("b", 0), ("h", 1), ("c", 1), ("out", 0),
             ("b", 1), ("h", 2), ("out", 1), ("c", 2), ("out", 2),
             ("b", 2), ("h", 3), ("out", 3), ("c", 3), ("b", 3)]
CHUNK_LOADS = [("ff1", 0), ("ff1", 1), ("ff2", 0), ("ff1", 2), ("ff2", 1), ("ff1", 3), ("ff2", 2), ("ff2", 3)]
N_MIX_LOADS = len(MIX_LOADS)
N_CHUNK_LOADS = len(CHUNK_LOADS)
assert N_CHUNK_LOADS % STAGES == 0

DOWN_BANKS = 4
G_PAIR = 0
G_PW = 4
G_POOL = G_PW + 8
G_CONV = G_POOL + 16
G_MLP = G_CONV + 16
UP_ORDER = [u for u in MIX_UNITS if u not in (("v", 0), ("v", 1), ("pw", 0))]
SIDE_UNITS = (("v", 3), ("c", 0))
S_MLP = 2 * len(UP_ORDER)
A_MLP = 16
N_CONV_BLOCKS = CONV // P
ROW_TAPS, ROW_SCALE, ROW_GAIN, N_ROWS = 0, 12, 16, 24
ROWS_BANK = 5
WARM_BANK = 4


def up_group(unit, half):
    return 2 * UP_ORDER.index(unit) + half


def load_number(c, pos):
    return N_MIX_LOADS + N_CHUNK_LOADS * c + pos


def build(nc, x, norm_mix_g, w_in, conv_w, pool_w, pool_scale, w_out, norm_mlp_g, w_ff1, w_ff2,
          norm_final_g, out):
    F32, F32R = mybir.dt.float32, mybir.dt.float32r
    ACT, ALU = mybir.ActivationFunctionType, mybir.AluOpType

    x_tiles = x[0].rearrange("(m p) d -> m p d", p=P)
    out_tiles = out[0].rearrange("(m p) d -> m p d", p=P)
    w_in_cols = w_in[0].rearrange("(k p) e -> p k e", p=P)
    w_ff1_cols = w_ff1[0].rearrange("(k p) e -> p k e", p=P)

    with ExitStack() as ctx:
        def sb(name, shape, dt=F32):
            return ctx.enter_context(nc.sbuf_tensor(name, shape, dt))

        def sem(name):
            return ctx.enter_context(nc.semaphore(name))

        stream = sb("stream", [P, TILES, D])
        xt_hi = sb("xt_hi", [P, DB, T], F32R)
        xt_lo = sb("xt_lo", [P, DB, T], F32R)
        act_hi = sb("act_hi", [P, KC, T], F32R)
        act_lo = sb("act_lo", [P, KC, T], F32R)
        down_hi = sb("down_hi", [P, KC, D], F32R)
        down_lo = sb("down_lo", [P, KC, D], F32R)
        up_hi = sb("up_hi", [P, UP_SLOTS, D], F32R)
        up_lo = sb("up_lo", [P, UP_SLOTS, D], F32R)
        raw = sb("raw", [P, STAGES, D])
        scratch = sb("scratch", [P, 3, PAD + T])
        ident = sb("ident", [P, P])
        inv_count = sb("inv_count", [P, WINDOWS[-1]])
        head = sb("head", [P, WINDOWS[-1]])
        rows = sb("rows", [N_ROWS, P])
        cols = sb("cols", [P, N_ROWS])
        ones = sb("ones", [P, P])
        warm = sb("warm", [P, HALF])
        rstd_row = sb("rstd_row", [P, T])
        sumsq = sb("sumsq", [P, 2, 3 * TILES])
        half_mean = sb("half_mean", [P, 3 * TILES])
        meansq = sb("meansq", [P, 3 * TILES])
        root = sb("root", [P, 3 * TILES])
        guess = sb("guess", [P, 3 * TILES])
        newton = sb("newton", [P, 2, 3 * TILES])
        rstd = sb("rstd", [P, 3 * TILES])
        psum = [ctx.enter_context(nc.psum_tensor(f"bank{b}", [P, HALF], F32)) for b in range(8)]

        row = [scratch[:, i, PAD:PAD + T] for i in range(3)]
        gain = row[2]
        squares = rstd_row
        diagonal = row[2].rearrange("p (m t) -> p m t", t=P)

        x_landed = [sem(f"x_landed{m}") for m in range(TILES)]
        raw_landed = [sem(f"raw_landed{s}") for s in range(STAGES)]
        gain_landed, rows_landed, stored = sem("gain_landed"), sem("rows_landed"), sem("stored")
        ident_zeroed, ident_ready, consts_ready = sem("ident_zeroed"), sem("ident_ready"), sem("consts_ready")
        cols_transposed, cols_ready = sem("cols_transposed"), sem("cols_ready")
        ones_ready, w_gained = sem("ones_ready"), sem("w_gained")
        diagonal_ready, rstd_spread, rstd_row_ready = sem("diagonal_ready"), sem("rstd_spread"), sem("rstd_row_ready")
        squared, mean_ready, root_ready = sem("squared"), sem("mean_ready"), sem("root_ready")
        table_loaded = sem("table_loaded")
        squared_late = sem("squared_late")
        half_mean_ready, h_ready = sem("half_mean_ready"), sem("h_ready")
        newton_step, rstd_ready, normed = sem("newton_step"), sem("rstd_ready"), sem("normed")
        transposed, xt_hi_ready, xt_ready = sem("transposed"), sem("xt_hi_ready"), sem("xt_ready")
        w_hi_ready, w_ready = sem("w_hi_ready"), sem("w_ready")
        up_done, down_done = sem("up_done"), sem("down_done")
        bank_read = [sem(f"bank_read{b}") for b in range(8)]
        window_added, head_ready, pooled = sem("window_added"), sem("head_ready"), sem("pooled")
        u_hi_ready, u_ready = sem("u_hi_ready"), sem("u_ready")
        tap_done, y_ready = sem("tap_done"), sem("y_ready")
        squared_relu = sem("squared_relu")
        act_hi_ready, act_ready = sem("act_hi_ready"), sem("act_ready")

        def in_side_bank(s):
            return s < S_MLP and UP_ORDER[s // 2] in SIDE_UNITS

        def up_bank(s):
            return (6 if in_side_bank(s) else 0) + s % 2

        def down_bank(g):
            return 2 + g % DOWN_BANKS

        def transpose_bank(norm, m, q):
            if norm == 0:
                return (6, 7, 0, 1)[(2 * m + q) % 4]
            return (2 if m == TILES - 1 else 6) + q

        def wait_group(eng, kind, base, step, c=0):
            eng.wait_ge(up_done if kind == "up" else down_done, base + 1 + step * c)

        def wait_bank_read(eng, kind, base, step, c=0):
            if kind == "up" and base < S_MLP and UP_ORDER[base // 2][0] == "b":
                eng.wait_ge(y_ready, 2 * UP_ORDER[base // 2][1] + base % 2 + 1)
            elif kind == "up":
                before = sum(up_bank(s) == up_bank(base) and (s >= S_MLP or UP_ORDER[s // 2][0] != "b")
                             for s in range(base))
                eng.wait_ge(bank_read[up_bank(base)], before + 1 + step // 2 * c)
            elif G_PW <= base < G_POOL:
                eng.wait_ge(act_ready, base - G_PW + 1)
            else:
                maps = 2 if base >= G_POOL else 0
                eng.wait_ge(bank_read[down_bank(base)], base // DOWN_BANKS - maps + 1 + step // DOWN_BANKS * c)

        def wait_unit(eng, unit):
            if unit == ("pw", 0):
                wait_group(eng, "down", G_PW + 7, 0)
            elif unit in UP_ORDER:
                wait_group(eng, "up", up_group(unit, 1), 0)
            else:
                wait_group(eng, "down", G_PAIR + 2 + unit[1], 0)

        def split_target(what):
            kind, j = what
            if kind in ("out", "ff2"):
                return down_hi[:, j % KC, :], down_lo[:, j % KC, :], D
            if kind == "ff1":
                slot = (len(MIX_UNITS) + j) % UP_SLOTS
            else:
                slot = MIX_UNITS.index(what) % UP_SLOTS
            width = KC * P if kind == "pw" else D
            return up_hi[:, slot, 0:width], up_lo[:, slot, 0:width], width

        block = ctx.enter_context(nc.Block())

        @block.sync
        def _(sp):
            def load(n0, per_chunk, what, c):
                kind, j = what
                slot = n0 % STAGES
                if n0 >= STAGES:
                    sp.wait_ge(w_ready, n0 - STAGES + 1 + per_chunk * c)
                dst = raw[:, slot, :]
                if kind == "out":
                    src = w_out[0, j * P:(j + 1) * P, :]
                elif kind == "ff2":
                    src = w_ff2[0, bass.ds(c * (KC * P) + j * P, P), :]
                elif kind == "ff1":
                    dst = dst.rearrange("p (k e) -> p k e", e=P)
                    src = w_ff1_cols[:, :, bass.ds(c * (KC * P) + j * P, P)]
                elif kind == "pw":
                    dst = dst[:, 0:KC * P].rearrange("p (g e) -> p g e", e=P)
                    src = pool_w[0].rearrange("g c e -> c g e")
                else:
                    e0 = MIX_COLUMN[kind] + j * P
                    dst = dst.rearrange("p (k e) -> p k e", e=P)
                    src = w_in_cols[:, :, e0:e0 + P]
                sp.dma_start(dst, src).then_inc(raw_landed[slot], 16)

            def load_gain(g):
                sp.dma_start(gain, g.partition_broadcast(P)).then_inc(gain_landed, 16)

            def load_tile(m):
                sp.dma_start(stream[:, m, :], x_tiles[m]).then_inc(x_landed[m], 16)

            load_tile(0)
            load_tile(1)
            load(0, 0, MIX_LOADS[0], 0)
            for m in range(2, 5):
                load_tile(m)
            load(1, 0, MIX_LOADS[1], 0)
            for m in range(5, TILES):
                load_tile(m)
            for n in range(2, N_MIX_LOADS):
                load(n, 0, MIX_LOADS[n], 0)
                if MIX_LOADS[n] == ("c", 1):
                    sp.wait_ge(u_ready, KC)
                    load_gain(norm_mlp_g[0])
            for pos in range(N_CHUNK_LOADS):
                load(load_number(0, pos), 0, CHUNK_LOADS[pos], 0)
            sp.wait_ge(normed, TILES)
            load_gain(norm_final_g)
            with sp.Fori(1, CHUNKS) as c:
                for pos in range(N_CHUNK_LOADS):
                    load(load_number(0, pos), N_CHUNK_LOADS, CHUNK_LOADS[pos], c)
            for m in range(TILES - 1):
                sp.wait_ge(normed, TILES + 2 * m + 2)
                sp.dma_start(out_tiles[m], stream[:, m, :]).then_inc(stored, 16)
            for half in range(2):
                part = slice(half * HALF, (half + 1) * HALF)
                sp.wait_ge(normed, TILES + 2 * (TILES - 1) + half + 1)
                sp.dma_start(out_tiles[TILES - 1, :, part], stream[:, TILES - 1, part]).then_inc(stored, 16)
            sp.wait_ge(stored, 16 * (TILES + 1))

        @block.gpsimd
        def _(pool):
            nc.gpsimd.memset(ones[:, :], 1.0).then_inc(ones_ready, 1)
            nc.gpsimd.memset(warm[:, :], 0.0).then_inc(ones_ready, 1)
            nc.gpsimd.memset(ident[:, :], 0.0).then_inc(ident_zeroed, 1)
            pool.wait_ge(ident_zeroed, 1)
            nc.gpsimd.affine_select(out=ident[:, :], in_=ident[:, :], compare_op=ALU.not_equal, fill=1.0,
                                    base=0, pattern=[[-1, P]], channel_multiplier=1).then_inc(ident_ready, 1)
            nc.gpsimd.memset(scratch[:, :, 0:PAD], 0.0).then_inc(consts_ready, 1)
            for t in range(WINDOWS[-1]):
                nc.gpsimd.memset(inv_count[:, t:t + 1], 1.0 / (t + 1)).then_inc(consts_ready, 1)
            pool.wait_ge(cols_ready, 1)
            for n, (kind, _) in enumerate(MIX_LOADS):
                if kind in MIX_COLUMN:
                    pool.wait_ge(raw_landed[n % STAGES], 16 * (n // STAGES + 1))
                    block_k = raw[:, n % STAGES, :].rearrange("p (k e) -> p k e", e=P)
                    nc.gpsimd.tensor_tensor(block_k, block_k,
                                            cols[:, ROW_GAIN:ROW_GAIN + DB].unsqueeze(2).to_broadcast([P, DB, P]),
                                            ALU.mult).then_inc(w_gained, 1)

        N_CONSTS = 1 + WINDOWS[-1]

        @block.scalar
        def _(act):
            def split_hi(what, n0, per_chunk=0, c=0):
                hi, _, width = split_target(what)
                if what[0] in MIX_COLUMN:
                    act.wait_ge(w_gained, sum(kind in MIX_COLUMN for kind, _ in MIX_LOADS[:n0]) + 1)
                else:
                    act.wait_ge(raw_landed[n0 % STAGES], 16 * (n0 // STAGES + 1) + 16 * (per_chunk // STAGES) * c)
                nc.scalar.activation(hi, raw[:, n0 % STAGES, 0:width], ACT.Copy).then_inc(w_hi_ready, 1)

            def split_mix_hi(what):
                n = MIX_LOADS.index(what)
                if what[0] != "out":
                    u = MIX_UNITS.index(what)
                    if u >= UP_SLOTS:
                        wait_unit(act, MIX_UNITS[u - UP_SLOTS])
                elif what[1] < KC:
                    wait_group(act, "down", G_CONV - 1, 0)
                split_hi(what, n)

            def root_of_mean(q, at):
                act.wait_ge(mean_ready, q + 1)
                nc.scalar.activation(root[:, at], meansq[:, at], ACT.Sqrt).then_inc(root_ready, 1)

            def root_mean_square(norm, m):
                i = norm * TILES + m
                base = G_CONV if norm == 1 else G_MLP + 16 * (CHUNKS - 1)
                for half in range(2):
                    part = slice(half * HALF, (half + 1) * HALF)
                    wait_bank_read(act, "down", base + 2 * m + half, 0)
                    if i > TILES:
                        act.wait_ge(squared, TILES // 2 + 2 * (i - TILES - 1) + half + 1)
                    nc.scalar.activation(squares[:, part], stream[:, m, part], ACT.Square,
                                         accum_out=sumsq[:, half, i:i + 1]).then_inc(squared, 1)
                root_of_mean(i - TILES + 1, slice(i, i + 1))

            def transpose_hi(norm, m):
                for q in range(2):
                    n = 2 * (norm * TILES + m) + q
                    act.wait_ge(transposed, n + 1)
                    nc.scalar.activation(xt_hi[:, 4 * q:4 * q + 4, m * P:(m + 1) * P],
                                         psum[transpose_bank(norm, m, q)][:, :].rearrange(
                                             "p (k t) -> p k t", t=P),
                                         ACT.Copy).then_inc(xt_hi_ready, 1)

            def sum_of_squares(m):
                act.wait_ge(x_landed[m], 16)
                if m >= 2:
                    act.wait_ge(squared, m - 1)
                nc.scalar.activation(row[m % 2], stream[:, m, :], ACT.Square,
                                     accum_out=sumsq[:, 0, m:m + 1]).then_inc(squared, 1)

            act.wait_ge(ones_ready, 1)
            nc.scalar.activation(root[:, 0:1], ones[:, 0:1], ACT.Sqrt).then_inc(table_loaded, 1)

            act.dma_start(rows[ROW_GAIN:ROW_GAIN + DB, :],
                          norm_mix_g[0].rearrange("(k p) -> k p", p=P)).then_inc(rows_landed, 16)
            act.dma_start(rows[ROW_TAPS:ROW_TAPS + 12, :],
                          conv_w[0].rearrange("t (j p) -> (t j) p", p=P)).then_inc(rows_landed, 16)
            act.dma_start(rows[ROW_SCALE:ROW_SCALE + 4, :],
                          pool_scale[0].rearrange("(j p) -> j p", p=P)).then_inc(rows_landed, 16)
            transpose_hi(0, 0)
            act.wait_ge(cols_transposed, 1)
            nc.scalar.activation(cols[:, :], psum[ROWS_BANK][:, 0:N_ROWS], ACT.Copy).then_inc(cols_ready, 1)
            transpose_hi(0, 1)
            transpose_hi(0, 2)
            split_mix_hi(("v", 0))
            transpose_hi(0, 3)
            sum_of_squares(0)
            sum_of_squares(1)
            split_mix_hi(("v", 1))
            transpose_hi(0, 4)
            sum_of_squares(2)
            transpose_hi(0, 5)
            sum_of_squares(3)
            transpose_hi(0, 6)
            transpose_hi(0, 7)
            act.wait_ge(table_loaded, 1)
            root_of_mean(0, slice(0, TILES))
            for half in range(2):
                act.wait_ge(rstd_spread, half + 1)
                nc.scalar.activation(rstd_row[:, half * HALF:(half + 1) * HALF], psum[6 + half][:, :],
                                     ACT.Copy).then_inc(rstd_row_ready, 1)

            split_mix_hi(("v", 2))
            for j in range(KC):
                if j >= 1:
                    split_mix_hi([("v", 3), ("h", 0), ("pw", 0)][j - 1])
                if j < 3:
                    split_mix_hi(("out", KC + j))
                if j == 3:
                    split_mix_hi(("c", 0))
                act.wait_ge(pooled, j + 1)
                nc.scalar.activation(act_hi[:, j, :], row[1 + j % 2], ACT.Copy).then_inc(u_hi_ready, 1)
            split_mix_hi(("out", 7))

            for j in range(N_CONV_BLOCKS):
                if j == 0:
                    for i in range(8):
                        g = G_PW + i
                        wait_group(act, "down", g, 0)
                        channel_scale = cols[:, ROW_SCALE + i // 2:ROW_SCALE + i // 2 + 1]
                        nc.scalar.activation(act_hi[:, i // 2, (i % 2) * HALF:(i % 2 + 1) * HALF],
                                             psum[down_bank(g)][:, :], ACT.Copy,
                                             scale=channel_scale).then_inc(act_hi_ready, 1)
                split_mix_hi(("b", j))
                if j < 3:
                    split_mix_hi(("h", j + 1))
                    if j >= 1:
                        split_mix_hi(("out", 2 * j - 1))
                else:
                    wait_unit(act, ("c", 3))
                    split_hi(CHUNK_LOADS[0], load_number(0, 0))
                for half in range(2):
                    act.wait_ge(y_ready, 2 * j + half + 1)
                    nc.scalar.activation(act_hi[:, j, half * HALF:(half + 1) * HALF],
                                         row[0][:, half * HALF:(half + 1) * HALF],
                                         ACT.Copy).then_inc(act_hi_ready, 1)
                if j < 3:
                    split_mix_hi(("c", j + 1))
                    if j < 2:
                        split_mix_hi(("out", 2 * j))
                else:
                    wait_unit(act, ("b", 3))
                    split_hi(CHUNK_LOADS[1], load_number(0, 1))

            for m in range(TILES):
                root_mean_square(1, m)
                if m >= 1:
                    transpose_hi(1, m - 1)

            def relu(c, i):
                k, half = i // 2, i % 2
                if not isinstance(c, int) or i >= 2:
                    act.wait_ge(squared_relu, i - 1 + 8 * c)
                wait_group(act, "up", S_MLP + i, 8, c)
                r = row[0][:, (i % 2) * HALF:(i % 2 + 1) * HALF]
                bank = up_bank(S_MLP + i)
                nc.scalar.activation(r, psum[bank][:, :], ACT.Relu).then_inc(bank_read[bank], 1)
                wait_bank_read(act, "up", S_MLP + i, 8, c)
                nc.scalar.activation(act_hi[:, k, half * HALF:(half + 1) * HALF], r,
                                     ACT.Square).then_inc(act_hi_ready, 1)

            def split_ff1(j, c):
                wait_group(act, "up", S_MLP + 2 * (j - 2) + 1, 8, c)
                pos = CHUNK_LOADS.index(("ff1", j))
                split_hi(("ff1", j), load_number(0, pos), N_CHUNK_LOADS, c)

            def split_ff2(k, c):
                pos = CHUNK_LOADS.index(("ff2", k))
                split_hi(("ff2", k), load_number(0, pos), N_CHUNK_LOADS, c)

            def split_next_ff1(c):
                for j in range(2):
                    wait_group(act, "up", S_MLP + 2 * (j + 2) + 1, 8, c)
                    split_hi(("ff1", j), load_number(1, j), N_CHUNK_LOADS, c)

            def chunk(c):
                wait_group(act, "down", G_MLP - 1, 16, c)
                for j in range(KC):
                    if j in (1, 2):
                        split_ff1(j + 1, c)
                    split_ff2(j, c)
                    relu(c, 2 * j)
                    relu(c, 2 * j + 1)

            transpose_hi(1, TILES - 1)
            chunk(0)
            split_next_ff1(0)
            with act.Fori(1, CHUNKS - 1) as c:
                chunk(c)
                split_next_ff1(c)
            chunk(CHUNKS - 1)
            for m in range(TILES):
                root_mean_square(2, m)

        @block.vector
        def _(dve):
            def split_lo(what, n0, per_chunk=0, c=0):
                hi, lo, width = split_target(what)
                dve.wait_ge(w_hi_ready, n0 + 1 + per_chunk * c)
                nc.vector.tensor_tensor(lo, raw[:, n0 % STAGES, 0:width], hi.bitcast(F32),
                                        ALU.subtract).then_inc(w_ready, 1)

            def split_mix_lo(what):
                split_lo(what, MIX_LOADS.index(what))

            def reciprocal_root(q, at):
                dve.wait_ge(root_ready, q + 1)
                nc.vector.reciprocal(guess[:, at], root[:, at]).then_inc(newton_step, 1)
                dve.wait_ge(newton_step, 4 * q + 1)
                nc.vector.tensor_tensor(newton[:, 0, at], guess[:, at], guess[:, at],
                                        ALU.mult).then_inc(newton_step, 1)
                dve.wait_ge(newton_step, 4 * q + 2)
                nc.vector.scalar_tensor_tensor(newton[:, 1, at], newton[:, 0, at], -0.5, meansq[:, at],
                                               ALU.mult, ALU.mult).then_inc(newton_step, 1)
                dve.wait_ge(newton_step, 4 * q + 3)
                nc.vector.tensor_scalar(newton[:, 0, at], newton[:, 1, at], 1.5, None,
                                        ALU.add).then_inc(newton_step, 1)
                dve.wait_ge(newton_step, 4 * q + 4)
                nc.vector.tensor_tensor(rstd[:, at], guess[:, at], newton[:, 0, at],
                                        ALU.mult).then_inc(rstd_ready, 1)
                dve.wait_ge(rstd_ready, q + 1)

            def normalise(norm, m):
                i = norm * TILES + m
                q = i - TILES + 1
                at = slice(i, i + 1)
                dve.wait_ge(squared, TILES // 2 + 2 * (q - 1) + 1)
                nc.vector.tensor_scalar(half_mean[:, at], sumsq[:, 0, at], 1.0 / D, EPS, ALU.mult,
                                        ALU.add).then_inc(half_mean_ready, 1)
                dve.wait_ge(half_mean_ready, q)
                dve.wait_ge(squared, TILES // 2 + 2 * (q - 1) + 2)
                nc.vector.scalar_tensor_tensor(meansq[:, at], sumsq[:, 1, at], 1.0 / D, half_mean[:, at],
                                               ALU.mult, ALU.add).then_inc(mean_ready, 1)
                reciprocal_root(q, at)
                if m == 0:
                    dve.wait_ge(gain_landed, 16 * norm)
                if norm == 1:
                    if m >= 2:
                        dve.wait_ge(transposed, 2 * TILES + 2 * (m - 1))
                    nc.vector.scalar_tensor_tensor(row[m % 2], stream[:, m, :], rstd[:, at], gain,
                                                   ALU.mult, ALU.mult).then_inc(normed, 1)
                else:
                    for half in range(2):
                        part = slice(half * HALF, (half + 1) * HALF)
                        nc.vector.scalar_tensor_tensor(stream[:, m, part], stream[:, m, part], rstd[:, at],
                                                       gain[:, part], ALU.mult, ALU.mult).then_inc(normed, 1)

            def transpose_lo(norm, m):
                for q in range(2):
                    n = 2 * (norm * TILES + m) + q
                    hi = xt_hi[:, 4 * q:4 * q + 4, m * P:(m + 1) * P]
                    dve.wait_ge(xt_hi_ready, n + 1)
                    nc.vector.tensor_tensor(xt_lo[:, 4 * q:4 * q + 4, m * P:(m + 1) * P],
                                            psum[transpose_bank(norm, m, q)][:, :].rearrange(
                                                "p (k t) -> p k t", t=P),
                                            hi.bitcast(F32), ALU.subtract).then_inc(xt_ready, 1)

            def add_group(base, i, c=0, first=False):
                g = base + i
                dst = stream[:, i // 2, (i % 2) * HALF:(i % 2 + 1) * HALF]
                if not first:
                    wait_bank_read(dve, "down", g - 16, 16, c)
                wait_group(dve, "down", g, 16, c)
                nc.vector.tensor_tensor(dst, psum[down_bank(g)][:, :], dst,
                                        ALU.add).then_inc(bank_read[down_bank(g)], 1)

            transpose_lo(0, 0)
            transpose_lo(0, 1)
            transpose_lo(0, 2)
            transpose_lo(0, 3)
            split_mix_lo(("v", 0))

            def sum_of_squares(m):
                dve.wait_ge(x_landed[m], 16)
                if m >= 5:
                    dve.wait_ge(squared_late, m - 4)
                nc.vector.tensor_tensor_reduce(out=row[2], in0=stream[:, m, :], in1=stream[:, m, :],
                                               scale=1.0, scalar=0.0, op0=ALU.mult, op1=ALU.add,
                                               accum_out=sumsq[:, 0, m:m + 1]).then_inc(squared_late, 1)

            sum_of_squares(4)
            split_mix_lo(("v", 1))
            transpose_lo(0, 4)
            transpose_lo(0, 5)
            sum_of_squares(5)
            transpose_lo(0, 6)
            sum_of_squares(6)
            transpose_lo(0, 7)
            sum_of_squares(7)
            dve.wait_ge(squared, 4)
            dve.wait_ge(squared_late, 4)
            nc.vector.tensor_scalar(meansq[:, 0:TILES], sumsq[:, 0, 0:TILES], 1.0 / D, EPS, ALU.mult,
                                    ALU.add).then_inc(mean_ready, 1)
            reciprocal_root(0, slice(0, TILES))
            dve.wait_ge(ident_ready, 1)
            for m in range(TILES):
                nc.vector.tensor_scalar(diagonal[:, m, :], ident[:, :], rstd[:, m:m + 1], None,
                                        ALU.mult).then_inc(diagonal_ready, 1)

            def from_psum(row_part, psum_part, rstd_part, done):
                nc.vector.tensor_tensor(row_part, psum_part, rstd_part, ALU.mult).then_inc(done, 1)

            dve.wait_ge(consts_ready, N_CONSTS)
            dve.wait_ge(rstd_row_ready, 2)
            added = 0
            for j in range(KC):
                w = WINDOWS[j]
                for half in range(2):
                    part = slice(half * HALF, (half + 1) * HALF)
                    kind, g = ("down", G_PAIR + 2 * half + j) if j < 2 else ("up", up_group(("v", j), half))
                    bank = down_bank(g) if j < 2 else up_bank(g)
                    wait_group(dve, kind, g, 0)
                    if j >= 1:
                        dve.wait_ge(pooled, j)
                    from_psum(row[0][:, part], psum[bank][:, :], rstd_row[:, part], bank_read[bank])
                for half in range(2):
                    if j < 2:
                        wait_bank_read(dve, "down", G_PAIR + 2 * half + j, 0)
                    else:
                        wait_bank_read(dve, "up", up_group(("v", j), half), 0)
                split_mix_lo([("v", 2), ("v", 3), ("h", 0), ("pw", 0)][j])
                if j >= 1:
                    dve.wait_ge(u_ready, j)
                src = 0
                for i in range(j + 1):
                    dst = 1 + i % 2
                    shift = 1 << i
                    nc.vector.tensor_tensor(row[dst], scratch[:, src, PAD:PAD + T],
                                            scratch[:, src, PAD - shift:PAD + T - shift],
                                            ALU.add).then_inc(window_added, 1)
                    added += 1
                    dve.wait_ge(window_added, added)
                    src = dst
                total, v = row[src], row[0]
                nc.vector.tensor_tensor(head[:, 0:w - 1], total[:, 0:w - 1], inv_count[:, 0:w - 1],
                                        ALU.mult).then_inc(head_ready, 1)
                dve.wait_ge(head_ready, 2 * j + 1)
                nc.vector.tensor_tensor(total[:, 0:w - 1], head[:, 0:w - 1], v[:, 0:w - 1],
                                        ALU.subtract).then_inc(head_ready, 1)
                dve.wait_ge(head_ready, 2 * j + 2)
                nc.vector.scalar_tensor_tensor(total[:, w - 1:T], total[:, w - 1:T], 1.0 / w, v[:, w - 1:T],
                                               ALU.mult, ALU.subtract).then_inc(pooled, 1)
                if j < 3:
                    split_mix_lo(("out", KC + j))
                else:
                    split_mix_lo(("c", 0))
                dve.wait_ge(u_hi_ready, j + 1)
                nc.vector.tensor_tensor(act_lo[:, j, :], total, act_hi[:, j, :].bitcast(F32),
                                        ALU.subtract).then_inc(u_ready, 1)

            def pooling_maps_lo(i0):
                for i in range(i0, i0 + 4):
                    g, part = G_PW + i, slice((i % 2) * HALF, (i % 2 + 1) * HALF)
                    dve.wait_ge(act_hi_ready, i + 1)
                    nc.vector.scalar_tensor_tensor(act_lo[:, i // 2, part], psum[down_bank(g)][:, :],
                                                   cols[:, ROW_SCALE + i // 2:ROW_SCALE + i // 2 + 1],
                                                   act_hi[:, i // 2, part].bitcast(F32),
                                                   ALU.mult, ALU.subtract).then_inc(act_ready, 1)

            dve.wait_ge(cols_ready, 1)
            for j in range(N_CONV_BLOCKS):
                for half in range(2):
                    part = slice(half * HALF, (half + 1) * HALF)
                    s = up_group(("h", j), half)
                    if j == 0:
                        dve.wait_ge(pooled, KC)
                    else:
                        dve.wait_ge(act_ready, 8 + 2 * j)
                    wait_group(dve, "up", s, 0)
                    from_psum(row[0][:, part], psum[up_bank(s)][:, :], rstd_row[:, part],
                              bank_read[up_bank(s)])
                if j == 0:
                    split_mix_lo(("out", 7))
                    pooling_maps_lo(0)
                for half in range(2):
                    part = slice(half * HALF, (half + 1) * HALF)
                    wait_bank_read(dve, "up", up_group(("h", j), half), 0)
                    nc.vector.tensor_tensor(row[0][:, part], row[0][:, part], rstd_row[:, part],
                                            ALU.mult).then_inc(h_ready, 1)
                if j == 0:
                    pooling_maps_lo(4)
                split_mix_lo(("b", j))
                for half in range(2):
                    part = slice(half * HALF, (half + 1) * HALF)
                    s = up_group(("c", j), half)
                    dve.wait_ge(h_ready, 2 * j + half + 1)
                    if half == 0 and j >= 1:
                        dve.wait_ge(tap_done, 8 * j)
                    wait_group(dve, "up", s, 0)
                    nc.vector.tensor_tensor(row[1][:, part], psum[up_bank(s)][:, :], row[0][:, part],
                                            ALU.mult).then_inc(bank_read[up_bank(s)], 1)
                if j == 0:
                    for i in range(16):
                        add_group(G_POOL, i, first=True)
                if j < 3:
                    split_mix_lo(("h", j + 1))
                    if j >= 1:
                        split_mix_lo(("out", 2 * j - 1))
                else:
                    split_lo(CHUNK_LOADS[0], load_number(0, 0))
                for half in range(2):
                    part = slice(half * HALF, (half + 1) * HALF)
                    wait_bank_read(dve, "up", up_group(("c", j), half), 0)
                    for tap in range(TAPS):
                        lag = TAPS - 1 - tap
                        z = scratch[:, 1, PAD + half * HALF - lag:PAD + (half + 1) * HALF - lag]
                        weight = cols[:, ROW_TAPS + 4 * tap + j:ROW_TAPS + 4 * tap + j + 1]
                        if tap == 0:
                            nc.vector.tensor_scalar(row[0][:, part], z, weight, None,
                                                    ALU.mult).then_inc(tap_done, 1)
                        else:
                            nc.vector.scalar_tensor_tensor(row[0][:, part], z, weight, row[0][:, part],
                                                           ALU.mult, ALU.add).then_inc(tap_done, 1)
                        dve.wait_ge(tap_done, 8 * j + 4 * half + tap + 1)
                    nc.vector.tensor_tensor(row[0][:, part], row[0][:, part], rstd_row[:, part],
                                            ALU.mult).then_inc(tap_done, 1)
                for half in range(2):
                    part = slice(half * HALF, (half + 1) * HALF)
                    s = up_group(("b", j), half)
                    dve.wait_ge(tap_done, 8 * j + 4 * half + 4)
                    wait_group(dve, "up", s, 0)
                    nc.vector.tensor_tensor(row[0][:, part], psum[up_bank(s)][:, :], row[0][:, part],
                                            ALU.mult).then_inc(y_ready, 1)
                    dve.wait_ge(y_ready, 2 * j + half + 1)
                    dve.wait_ge(act_hi_ready, 8 + 2 * j + half + 1)
                    nc.vector.tensor_tensor(act_lo[:, j, part], row[0][:, part],
                                            act_hi[:, j, part].bitcast(F32),
                                            ALU.subtract).then_inc(act_ready, 1)
                if j < 3:
                    split_mix_lo(("c", j + 1))
                    if j < 2:
                        split_mix_lo(("out", 2 * j))

            for m in range(TILES):
                add_group(G_CONV, 2 * m)
                add_group(G_CONV, 2 * m + 1)
                normalise(1, m)
                if m == 0:
                    split_lo(CHUNK_LOADS[1], load_number(0, 1))
                if m >= 1:
                    transpose_lo(1, m - 1)

            def square(c, i):
                k, half = i // 2, i % 2
                part = slice(half * HALF, (half + 1) * HALF)
                side = slice((i % 2) * HALF, (i % 2 + 1) * HALF)
                wait_bank_read(dve, "up", S_MLP + i, 8, c)
                if not isinstance(c, int) or i >= 2:
                    dve.wait_ge(act_ready, A_MLP - 1 + i + 8 * c)
                nc.vector.tensor_tensor(row[1][:, side], row[0][:, side], row[0][:, side],
                                        ALU.mult).then_inc(squared_relu, 1)
                dve.wait_ge(squared_relu, i + 1 + 8 * c)
                dve.wait_ge(act_hi_ready, A_MLP + i + 1 + 8 * c)
                nc.vector.tensor_tensor(act_lo[:, k, part], row[1][:, side], act_hi[:, k, part].bitcast(F32),
                                        ALU.subtract).then_inc(act_ready, 1)

            def split_chunk_lo(what, c):
                split_lo(what, load_number(0, CHUNK_LOADS.index(what)), N_CHUNK_LOADS, c)

            def down(c):
                for i in range(16):
                    add_group(G_MLP, i, c)
                    if i in (2, 4):
                        j = i // 2 - 1
                        split_lo(("ff1", j), load_number(1, j), N_CHUNK_LOADS, c)

            def chunk(c):
                for j in range(KC):
                    if j in (1, 2):
                        split_chunk_lo(("ff1", j + 1), c)
                    split_chunk_lo(("ff2", j), c)
                    square(c, 2 * j)
                    square(c, 2 * j + 1)

            transpose_lo(1, TILES - 1)
            chunk(0)
            down(0)
            with dve.Fori(1, CHUNKS - 1) as c:
                chunk(c)
                down(c)
            chunk(CHUNKS - 1)
            for m in range(TILES):
                add_group(G_MLP, 2 * m, CHUNKS - 1)
                add_group(G_MLP, 2 * m + 1, CHUNKS - 1)
                normalise(2, m)

        @block.tensor
        def _(pe):
            def products(dst, stationary, moving, first, last):
                (s_hi, s_lo), (m_hi, m_lo) = stationary, moving
                nc.tensor.matmul(dst, s_hi, m_hi, start=first, stop=False)
                nc.tensor.matmul(dst, s_hi, m_lo, start=False, stop=False)
                return nc.tensor.matmul(dst, s_lo, m_hi, start=False, stop=last)

            def transpose_tile(norm, m):
                if norm == 0:
                    pe.wait_ge(x_landed[m], 16)
                else:
                    pe.wait_ge(normed, m + 1)
                for q in range(2):
                    n = 2 * (norm * TILES + m) + q
                    reuse = 4 if norm == 0 else 2
                    if norm == 1 and m == TILES - 1:
                        wait_bank_read(pe, "down", G_CONV + 12 + q, 0)
                    elif n >= reuse:
                        pe.wait_ge(xt_ready, n - reuse + 1)
                    for k in range(4):
                        at = (4 * q + k) * P
                        src = stream[:, m, at:at + P] if norm == 0 else row[m % 2][:, at:at + P]
                        last = nc.tensor.transpose(psum[transpose_bank(norm, m, q)][:, k * P:(k + 1) * P],
                                                   src, ident[:, :])
                    last.then_inc(transposed, 1)

            def wait_bank_free(kind, base, step=0, c=0):
                if kind == "down":
                    before = base - DOWN_BANKS
                else:
                    before = max((s for s in range(base) if up_bank(s) == up_bank(base)), default=-1)
                if before >= 0:
                    wait_bank_read(pe, kind, before, step, c)
                elif kind == "up" and in_side_bank(base):
                    pe.wait_ge(rstd_row_ready, base % 2 + 1)

            def up_product(slot, half, bank, done, between={}):
                for k in range(DB):
                    if k in between:
                        between[k]()
                    cols_k = slice(k * P, (k + 1) * P)
                    part = slice(half * HALF, (half + 1) * HALF)
                    last = products(psum[bank][:, :],
                                    (up_hi[:, slot, cols_k], up_lo[:, slot, cols_k]),
                                    (xt_hi[:, k, part], xt_lo[:, k, part]), k == 0, k == DB - 1)
                last.then_inc(done, 1)

            def mix_up(unit, half):
                s = up_group(unit, half)
                if half == 0:
                    pe.wait_ge(w_ready, MIX_LOADS.index(unit) + 1)
                wait_bank_free("up", s)
                up_product(MIX_UNITS.index(unit) % UP_SLOTS, half, up_bank(s), up_done)

            def down_product(base, i, c, weight_load, act_base):
                g, m, n = base + i, i // 2, i % 2
                wait_bank_free("down", g, 16, c)
                for k in range(KC):
                    if i == 0:
                        load0, per_chunk = weight_load(k)
                        pe.wait_ge(w_ready, load0 + 1 + per_chunk * c)
                    if i in (0, TILES):
                        pe.wait_ge(act_ready, act_base + 2 * k + i // TILES + 1 + 8 * c)
                    last = products(psum[down_bank(g)][:, :],
                                    (act_hi[:, k, m * P:(m + 1) * P], act_lo[:, k, m * P:(m + 1) * P]),
                                    (down_hi[:, k, n * HALF:(n + 1) * HALF],
                                     down_lo[:, k, n * HALF:(n + 1) * HALF]), k == 0, k == KC - 1)
                last.then_inc(down_done, 1)

            def transpose_rows():
                pe.wait_ge(rows_landed, 48)
                nc.tensor.transpose(psum[ROWS_BANK][:, 0:N_ROWS], rows[:, :],
                                    ident[0:N_ROWS, 0:N_ROWS]).then_inc(cols_transposed, 1)

            def warm_up(n):
                for _ in range(n):
                    nc.tensor.matmul(psum[WARM_BANK][:, :], ones[:, :], warm[:, :], start=True, stop=True)

            pe.wait_ge(ones_ready, 2)
            warm_up(2)
            pe.wait_ge(ident_ready, 1)

            def wait_stream(norm, half, q):
                pe.wait_ge(xt_ready, 2 * TILES * norm + 8 * half + 7 + q)

            def pair(j, half, between={}):
                if half == 0:
                    pe.wait_ge(w_ready, MIX_LOADS.index(("v", j)) + 1)
                wait_stream(0, half, 0)
                between = {4: lambda: wait_stream(0, half, 1), **between}
                up_product(j, half, down_bank(G_PAIR + 2 * half + j), down_done, between)

            def first_group():
                def sweep(weights, stream_t, tokens, first=False, last=False):
                    for k in range(DB):
                        done = nc.tensor.matmul(psum[down_bank(G_PAIR)][:, tokens],
                                                weights[:, 0, k * P:(k + 1) * P], stream_t[:, k, tokens],
                                                start=first and k == 0, stop=last and k == DB - 1)
                    return done

                pe.wait_ge(w_hi_ready, 1)
                for m in (0, 2):
                    pe.wait_ge(xt_hi_ready, 2 * (m + 2))
                    sweep(up_hi, xt_hi, slice(m * P, (m + 2) * P), first=m == 0)
                transpose_tile(0, 4)
                pe.wait_ge(xt_ready, 8)
                sweep(up_hi, xt_lo, slice(0, HALF))
                transpose_tile(0, 5)
                pe.wait_ge(w_ready, 1)
                sweep(up_lo, xt_hi, slice(0, HALF), last=True).then_inc(down_done, 1)

            def spread_rstd():
                pe.wait_ge(ones_ready, 1)
                pe.wait_ge(xt_ready, 2 * TILES)
                pe.wait_ge(diagonal_ready, TILES)
                for m in range(TILES):
                    last = nc.tensor.matmul(psum[6 + m // 4][:, (m % 4) * P:(m % 4 + 1) * P], ones[:, :],
                                            diagonal[:, m, :], start=True, stop=True)
                    if m % 4 == 3:
                        last.then_inc(rstd_spread, 1)

            for m in range(4):
                transpose_tile(0, m)
                if m == 0:
                    transpose_rows()
            first_group()
            pair(1, 0, {1: lambda: transpose_tile(0, 6), 3: lambda: transpose_tile(0, 7)})
            pair(0, 1, {7: spread_rstd})
            pe.wait_ge(cols_ready, 1)
            pair(1, 1)
            for unit in MIX_UNITS[2:5]:
                for half in range(2):
                    mix_up(unit, half)

            def pooling_maps(i0):
                slot = MIX_UNITS.index(("pw", 0)) % UP_SLOTS
                for i in range(i0, i0 + 4):
                    g, j, part = G_PW + i, i // 2, slice((i % 2) * HALF, (i % 2 + 1) * HALF)
                    wait_bank_free("down", g)
                    pe.wait_ge(u_ready, j + 1)
                    products(psum[down_bank(g)][:, :],
                             (up_hi[:, slot, j * P:(j + 1) * P], up_lo[:, slot, j * P:(j + 1) * P]),
                             (act_hi[:, j, part], act_lo[:, j, part]), True, True).then_inc(down_done, 1)

            pe.wait_ge(w_ready, MIX_LOADS.index(("pw", 0)) + 1)
            pooling_maps(0)
            mix_up(("c", 0), 0)
            pooling_maps(4)
            mix_up(("c", 0), 1)
            for i in range(16):
                down_product(G_POOL, i, 0, lambda k: (MIX_LOADS.index(("out", KC + k)), 0), 0)
            for unit in MIX_UNITS[7:]:
                for half in range(2):
                    mix_up(unit, half)
            for m in range(TILES):
                for n in range(2):
                    down_product(G_CONV, 2 * m + n, 0, lambda k: (MIX_LOADS.index(("out", k)), 0), 8)
                if m >= 1:
                    transpose_tile(1, m - 1)

            def mlp_up(i, c, between={}):
                j, half = i // 2, i % 2
                if half == 0:
                    pos = CHUNK_LOADS.index(("ff1", j))
                    pe.wait_ge(w_ready, load_number(0, pos) + 1 + N_CHUNK_LOADS * c)
                wait_bank_free("up", S_MLP + i, 8, c)
                up_product((len(MIX_UNITS) + j) % UP_SLOTS, half, up_bank(S_MLP + i), up_done, between)

            def mlp_down(c):
                for i in range(16):
                    down_product(G_MLP, i, c,
                                 lambda k: (load_number(0, CHUNK_LOADS.index(("ff2", k))), N_CHUNK_LOADS),
                                 A_MLP)

            pe.wait_ge(xt_ready, 2 * TILES + 8)
            mlp_up(0, 0, {6: lambda: transpose_tile(1, TILES - 1)})
            wait_stream(1, 1, 0)
            mlp_up(1, 0, {4: lambda: wait_stream(1, 1, 1)})
            for i in range(2, 8):
                mlp_up(i, 0)
            mlp_down(0)
            with pe.Fori(1, CHUNKS) as c:
                for i in range(8):
                    mlp_up(i, c)
                mlp_down(c)


_INS = ["x", "norm_mix_g", "w_in", "conv_w", "pool_w", "pool_scale", "w_out", "norm_mlp_g", "w_ff1", "w_ff2",
        "norm_final_g"]


def kernel(**inputs):
    import numpy as _np
    import concourse.bacc as _bacc
    from concourse import mybir as _mybir
    from concourse.bass_utils import run_bass_kernel_spmd as _run

    nc = _bacc.Bacc("TRN2", target_bir_lowering=False, num_devices=1,
                     dynamic_dma_scratch_size=1024)
    arrays, args = {}, []
    for name in _INS:
        a = _np.ascontiguousarray(inputs[name])
        arrays[f"in_{name}"] = a
        args.append(nc.dram_tensor(f"in_{name}", a.shape, _mybir.dt.from_np(a.dtype), kind="ExternalInput").ap())
    args.append(nc.dram_tensor("out_y", (1, T, D), _mybir.dt.float32, kind="ExternalOutput").ap())
    build(nc, *args)
    r = _run(nc, [arrays], core_ids=[0])
    return r.results[0]["out_y"]
```
